# Optimizing a Trainium2 kernel written in Bass

```python
import jax, jax.numpy as jnp
from jax import lax
import numpy as np

D_MODEL = 1024
BATCH = 1
SEQ = 512
DEPTH = 2

RET_HEADS = 4
RET_DV = D_MODEL // (2 * RET_HEADS)
RET_DK = RET_DV // 2
RET_CHUNK = 128
ROPE_BASE = 10000.0
LRU_WIDTH = D_MODEL // 2
LRU_BLOCKS = 4
LRU_BW = LRU_WIDTH // LRU_BLOCKS
LRU_CONV = 4
LRU_C = 8.0
HG_HEADS = 8
HG_DK = D_MODEL // HG_HEADS
HG_DV = D_MODEL // HG_HEADS
HG_CHUNK = 32
N_EXPERTS = 16
N_GROUPS = 4
EXPERTS_PER_GROUP = N_EXPERTS // N_GROUPS
TOP_K = 2
D_EXPERT = 512
MOE_BLOCK = 128
DN_ALPHA = (2.0 * DEPTH) ** 0.25
DN_BETA = (8.0 * DEPTH) ** -0.25
N_EVEN = (DEPTH + 1) // 2
N_ODD = DEPTH // 2
LN_EPS = 1e-5
RMS_EPS = 1e-6
EVEN_SPLITS = (RET_HEADS * RET_DK,
               2 * RET_HEADS * RET_DK,
               2 * RET_HEADS * RET_DK + RET_HEADS * RET_DV,
               2 * RET_HEADS * RET_DK + 2 * RET_HEADS * RET_DV,
               2 * RET_HEADS * RET_DK + 2 * RET_HEADS * RET_DV + LRU_WIDTH)
EVEN_IN = 2 * RET_HEADS * RET_DK + 2 * RET_HEADS * RET_DV + 2 * LRU_WIDTH
EVEN_OUT = RET_HEADS * RET_DV + LRU_WIDTH
ODD_IN = 5 * D_MODEL

kernel_name = 'hybrid_retention_rglru_hgrn2_grouped_moe_encoder'

def _layer_norm(x, w, b):
    xf = x.astype(jnp.float32)
    mu = jnp.mean(xf, axis=-1, keepdims=True)
    var = jnp.mean(jnp.square(xf - mu), axis=-1, keepdims=True)
    return ((xf - mu) * lax.rsqrt(var + LN_EPS) * w + b).astype(x.dtype)

def _head_norm(x):
    mu = jnp.mean(x, axis=-1, keepdims=True)
    var = jnp.mean(jnp.square(x - mu), axis=-1, keepdims=True)
    return (x - mu) * lax.rsqrt(var + LN_EPS)

def _rms_norm(x, w):
    return x * lax.rsqrt(jnp.mean(jnp.square(x), axis=-1, keepdims=True) + RMS_EPS) * w.astype(jnp.float32)

def _rotary(x, pos):
    d = x.shape[-1]
    inv_freq = ROPE_BASE ** (-jnp.arange(0, d, 2, dtype=jnp.float32) / d)
    ang = pos.astype(jnp.float32)[:, None] * inv_freq[None, :]
    cos = jnp.cos(ang)[None, :, None, :]
    sin = jnp.sin(ang)[None, :, None, :]
    x1, x2 = x[..., 0::2], x[..., 1::2]
    return jnp.stack([x1 * cos - x2 * sin, x1 * sin + x2 * cos], axis=-1).reshape(x.shape)

def _retention_bidir(q, k, v):
    B, S, H, dk = q.shape
    dv = v.shape[-1]
    C = RET_CHUNK
    N = S // C
    log_gamma = jnp.log1p(-(2.0 ** (-5.0 - jnp.arange(H, dtype=jnp.float32))))
    qc = (q * dk ** -0.5).reshape(B, N, C, H, dk)
    kc = k.reshape(B, N, C, H, dk)
    vc = v.reshape(B, N, C, H, dv)
    idx = jnp.arange(C, dtype=jnp.float32)
    d_intra = jnp.exp(log_gamma[:, None, None] * jnp.abs(idx[:, None] - idx[None, :]))
    scores = jnp.einsum('bnihd,bnjhd->bnhij', qc, kc) * d_intra
    o = jnp.einsum('bnhij,bnjhe->bnihe', scores, vc)
    q_dec_f = jnp.exp(log_gamma[None, :] * (idx[:, None] + 1.0))
    k_dec_f = jnp.exp(log_gamma[None, :] * (C - 1.0 - idx[:, None]))
    q_dec_b = jnp.exp(log_gamma[None, :] * (C - idx[:, None]))
    k_dec_b = jnp.exp(log_gamma[None, :] * idx[:, None])
    chunk_dec = jnp.exp(log_gamma * C)[None, :, None, None]
    kv_f = jnp.einsum('bnjhd,jh,bnjhe->nbhde', kc, k_dec_f, vc)
    kv_b = jnp.einsum('bnjhd,jh,bnjhe->nbhde', kc, k_dec_b, vc)

    def step(state, kv):
        return state * chunk_dec + kv, state

    init = jnp.zeros((B, H, dk, dv), jnp.float32)
    _, st_f = lax.scan(step, init, kv_f)
    _, st_b = lax.scan(step, init, kv_b, reverse=True)
    o = (o + jnp.einsum('bnihd,ih,nbhde->bnihe', qc, q_dec_f, st_f)
           + jnp.einsum('bnihd,ih,nbhde->bnihe', qc, q_dec_b, st_b))
    return o.reshape(B, S, H, dv)

def _rglru_bidir(x, conv_w, conv_b, gate_w, gate_b, lam):
    B, S, W = x.shape
    lo = LRU_CONV // 2
    hi = LRU_CONV - 1 - lo
    xc = lax.conv_general_dilated(x, conv_w.astype(jnp.float32)[:, None, :], window_strides=(1,),
                                  padding=[(lo, hi)], dimension_numbers=('NWC', 'WIO', 'NWC'),
                                  feature_group_count=W) + conv_b.astype(jnp.float32)
    xb = xc.reshape(B, S, LRU_BLOCKS, LRU_BW)
    gates = jax.nn.sigmoid(jnp.einsum('bsnc,zgncd->zgbsnd', xb, gate_w.astype(jnp.float32))
                           + gate_b.astype(jnp.float32)[:, :, None, None])
    gates = gates.reshape(2, 2, B, S, W)
    r, i = gates[:, 0], gates[:, 1]
    log_a = -LRU_C * r * jax.nn.softplus(-lam.astype(jnp.float32))[:, None, None, :]
    a = jnp.exp(log_a)
    b = jnp.sqrt(-jnp.expm1(2.0 * log_a)) * (i * xc[None])

    def comb(left, right):
        a1, b1 = left
        a2, b2 = right
        return a1 * a2, a2 * b1 + b2

    _, h_f = lax.associative_scan(comb, (a[0], b[0]), axis=1)
    _, h_b = lax.associative_scan(comb, (a[1], b[1]), axis=1, reverse=True)
    return h_f + h_b

def _gla_chunks(q, k, v, log_f):
    B, S, H, dk = q.shape
    dv = v.shape[-1]
    C = HG_CHUNK
    N = S // C

    def to_chunks(t):
        return t.reshape(B, N, C, H, t.shape[-1]).transpose(1, 0, 3, 2, 4)

    causal = jnp.tril(jnp.ones((C, C), dtype=bool))[:, :, None]

    def step(state, inp):
        qc, kc, vc, gc = inp
        b = jnp.cumsum(gc, axis=2)
        diff = b[:, :, :, None, :] - b[:, :, None, :, :]
        decay = jnp.exp(jnp.where(causal, diff, -jnp.inf))
        attn = jnp.einsum('bhid,bhjd,bhijd->bhij', qc, kc, decay)
        o = (jnp.einsum('bhij,bhje->bhie', attn, vc)
             + jnp.einsum('bhid,bhde->bhie', qc * jnp.exp(b), state))
        b_last = b[:, :, -1]
        new_state = (state * jnp.exp(b_last)[..., None]
                     + jnp.einsum('bhjd,bhje->bhde', kc * jnp.exp(b_last[:, :, None, :] - b), vc))
        return new_state, o

    init = jnp.zeros((B, H, dk, dv), jnp.float32)
    _, o = lax.scan(step, init, (to_chunks(q), to_chunks(k), to_chunks(v), to_chunks(log_f)))
    return o.transpose(1, 0, 3, 2, 4).reshape(B, S, H, dv)

def _even_mixer(h, w_in, w_out, conv_w, conv_b, gate_w, gate_b, lam):
    B, S, _ = h.shape
    proj = (h @ w_in).astype(jnp.float32)
    q, k, v, g, xr, gr = jnp.split(proj, list(EVEN_SPLITS), axis=-1)
    pos = jnp.arange(S)
    q = _rotary(q.reshape(B, S, RET_HEADS, RET_DK), pos)
    k = _rotary(k.reshape(B, S, RET_HEADS, RET_DK), pos)
    v = v.reshape(B, S, RET_HEADS, RET_DV)
    ret = _head_norm(_retention_bidir(q, k, v)).reshape(B, S, RET_HEADS * RET_DV)
    ret_out = jax.nn.silu(g) * ret
    lru_out = _rglru_bidir(xr, conv_w, conv_b, gate_w, gate_b, lam) * jax.nn.gelu(gr)
    return jnp.concatenate([ret_out, lru_out], axis=-1).astype(h.dtype) @ w_out

def _odd_mixer(h, w_in, w_out, lower_bounds, norm_w, layer):
    B, S, _ = h.shape
    proj = (h @ w_in).astype(jnp.float32)
    q, v, z_f, z_b, g = jnp.split(proj, 5, axis=-1)
    lb_all = jnp.cumsum(jax.nn.softmax(lower_bounds.astype(jnp.float32), axis=0), axis=0)
    lb = lb_all[layer] - lb_all[0]

    def heads(t):
        return t.reshape(B, S, HG_HEADS, -1)

    def forget(z):
        log_f = jnp.logaddexp(jnp.log(lb), jnp.log1p(-lb) + jax.nn.log_sigmoid(z))
        key = (1.0 - lb) * jax.nn.sigmoid(-z)
        return heads(log_f), heads(key)

    qh = heads(jax.nn.silu(q)) * HG_DK ** -0.5
    vh = heads(v)
    lf_f, k_f = forget(z_f)
    lf_b, k_b = forget(z_b)
    o_f = _gla_chunks(qh, k_f, vh, lf_f)
    flip = lambda t: jnp.flip(t, axis=1)
    o_b = flip(_gla_chunks(flip(qh), flip(k_b), flip(vh), flip(lf_b)))
    o = _rms_norm((o_f + o_b).reshape(B, S, HG_HEADS * HG_DV), norm_w) * jax.nn.silu(g)
    return o.astype(h.dtype) @ w_out

def _moe(h, router_w, w_gate, w_up, w_down):
    B, S, D = h.shape
    T = B * S
    x = h.reshape(T, D)
    probs = jax.nn.softmax((x @ router_w).astype(jnp.float32), axis=-1)
    top_v, top_i = lax.top_k(probs.reshape(T, N_GROUPS, EXPERTS_PER_GROUP), TOP_K)
    g_sel = jnp.argmax(jnp.sum(top_v, axis=-1), axis=-1)
    tok = jnp.arange(T, dtype=jnp.int32)
    vals = top_v[tok, g_sel]
    eidx = top_i[tok, g_sel] + g_sel[:, None].astype(jnp.int32) * EXPERTS_PER_GROUP
    gates = vals / jnp.sum(vals, axis=-1, keepdims=True)
    A = T * TOP_K
    flat_e = eidx.reshape(A).astype(jnp.int32)
    flat_tok = jnp.repeat(tok, TOP_K)
    flat_g = gates.reshape(A)
    order = jnp.argsort(flat_e)
    se = flat_e[order]
    counts = jnp.bincount(flat_e, length=N_EXPERTS).astype(jnp.int32)
    padded = (counts + MOE_BLOCK - 1) // MOE_BLOCK * MOE_BLOCK
    start = jnp.cumsum(counts) - counts
    ends_p = jnp.cumsum(padded)
    pstart = ends_p - padded
    dest = pstart[se] + jnp.arange(A, dtype=jnp.int32) - start[se]
    P = (A + MOE_BLOCK - 1) // MOE_BLOCK * MOE_BLOCK + N_EXPERTS * MOE_BLOCK
    nb = P // MOE_BLOCK
    buf_tok = jnp.zeros((P,), jnp.int32).at[dest].set(flat_tok[order])
    buf_gate = jnp.zeros((P,), jnp.float32).at[dest].set(flat_g[order])
    block_start = jnp.arange(nb, dtype=jnp.int32) * MOE_BLOCK
    block_e = jnp.minimum(jnp.searchsorted(ends_p, block_start, side='right'), N_EXPERTS - 1)
    xb = x[buf_tok].reshape(nb, MOE_BLOCK, D)

    def expert_block(args):
        xblk, e = args
        hid = jax.nn.silu(xblk @ w_gate[e]) * (xblk @ w_up[e])
        return hid @ w_down[e]

    yb = lax.map(expert_block, (xb, block_e)).reshape(P, D)
    y = jnp.zeros((T, D), h.dtype).at[buf_tok].add(yb * buf_gate[:, None].astype(yb.dtype))
    return y.reshape(B, S, D)

def setup_inputs(seed: int = 0) -> dict:
    key = jax.random.key(seed)
    ks = jax.random.split(key, 18)
    f32 = jnp.float32

    def nrm(k, shape, scale):
        return jax.random.normal(k, shape, f32) * scale

    x = nrm(ks[0], (BATCH, SEQ, D_MODEL), 1.0)
    w_in_even = nrm(ks[1], (N_EVEN, D_MODEL, EVEN_IN), D_MODEL ** -0.5)
    w_out_even = nrm(ks[2], (N_EVEN, EVEN_OUT, D_MODEL), EVEN_OUT ** -0.5 * DN_BETA)
    lru_conv_w = nrm(ks[3], (N_EVEN, LRU_CONV, LRU_WIDTH), LRU_CONV ** -0.5)
    lru_conv_b = nrm(ks[4], (N_EVEN, LRU_WIDTH), 0.01)
    lru_gate_w = nrm(ks[5], (N_EVEN, 2, 2, LRU_BLOCKS, LRU_BW, LRU_BW), LRU_BW ** -0.5)
    lru_gate_b = nrm(ks[6], (N_EVEN, 2, 2, LRU_BLOCKS, LRU_BW), 0.01)
    u = jax.random.uniform(ks[7], (N_EVEN, 2, LRU_WIDTH), f32, 0.9, 0.999)
    a = u ** (1.0 / LRU_C)
    lru_lambda = jnp.log(a) - jnp.log1p(-a)
    w_in_odd = nrm(ks[8], (N_ODD, D_MODEL, ODD_IN), D_MODEL ** -0.5)
    w_out_odd = nrm(ks[9], (N_ODD, HG_HEADS * HG_DV, D_MODEL), (HG_HEADS * HG_DV) ** -0.5 * DN_BETA)
    hg_lower_bounds = nrm(ks[10], (DEPTH, HG_HEADS * HG_DK), 0.5)
    hg_norm_w = 1.0 + nrm(ks[11], (N_ODD, HG_HEADS * HG_DV), 0.02)
    ln_w = 1.0 + nrm(ks[12], (DEPTH, 2, D_MODEL), 0.02)
    ln_b = nrm(ks[13], (DEPTH, 2, D_MODEL), 0.02)
    router_w = nrm(ks[14], (D_MODEL, N_EXPERTS), D_MODEL ** -0.5)
    moe_w_gate = nrm(ks[15], (DEPTH, N_EXPERTS, D_MODEL, D_EXPERT), D_MODEL ** -0.5)
    moe_w_up = nrm(ks[16], (DEPTH, N_EXPERTS, D_MODEL, D_EXPERT), D_MODEL ** -0.5)
    moe_w_down = nrm(ks[17], (DEPTH, N_EXPERTS, D_EXPERT, D_MODEL), D_EXPERT ** -0.5 * DN_BETA)
    return {'x': x, 'w_in_even': w_in_even, 'w_out_even': w_out_even,
            'lru_conv_w': lru_conv_w, 'lru_conv_b': lru_conv_b,
            'lru_gate_w': lru_gate_w, 'lru_gate_b': lru_gate_b, 'lru_lambda': lru_lambda,
            'w_in_odd': w_in_odd, 'w_out_odd': w_out_odd,
            'hg_lower_bounds': hg_lower_bounds, 'hg_norm_w': hg_norm_w,
            'ln_w': ln_w, 'ln_b': ln_b, 'router_w': router_w,
            'moe_w_gate': moe_w_gate, 'moe_w_up': moe_w_up, 'moe_w_down': moe_w_down}

def reference(x, w_in_even, w_out_even, lru_conv_w, lru_conv_b, lru_gate_w, lru_gate_b,
              lru_lambda, w_in_odd, w_out_odd, hg_lower_bounds, hg_norm_w, ln_w, ln_b,
              router_w, moe_w_gate, moe_w_up, moe_w_down):
    h = x
    for layer in range(DEPTH):
        j = layer // 2
        if layer % 2 == 0:
            y = _even_mixer(h, w_in_even[j], w_out_even[j], lru_conv_w[j], lru_conv_b[j],
                            lru_gate_w[j], lru_gate_b[j], lru_lambda[j])
        else:
            y = _odd_mixer(h, w_in_odd[j], w_out_odd[j], hg_lower_bounds, hg_norm_w[j], layer)
        h = _layer_norm(DN_ALPHA * h + y, ln_w[layer, 0], ln_b[layer, 0])
        y = _moe(h, router_w, moe_w_gate[layer], moe_w_up[layer], moe_w_down[layer])
        h = _layer_norm(DN_ALPHA * h + y, ln_w[layer, 1], ln_b[layer, 1])
    return h


_drawn_inputs = setup_inputs


def setup_inputs(seed=0):
    import zlib

    import numpy as np

    out = dict(_drawn_inputs(seed))
    spreads = {}
    factors = {'lru_gate_b': 8.0, 'hg_norm_w': 5.338}
    for name, (base, spread) in spreads.items():
        noise = np.random.default_rng([zlib.crc32(name.encode()), seed]).standard_normal(out[name].shape)
        drawn = base * np.exp(spread * noise) if base else spread * noise
        out[name] = __import__('jax').numpy.asarray(drawn.astype(out[name].dtype))
    for name, factor in factors.items():
        out[name] = (out[name] * factor).astype(out[name].dtype)
    return out
```

```python
from contextlib import ExitStack

import numpy as np
import concourse.bass as bass
from concourse import mybir

F32 = mybir.dt.float32
I32 = mybir.dt.int32
U32 = mybir.dt.uint32
ALU = mybir.AluOpType
ACT = mybir.ActivationFunctionType
AX = mybir.AxisListType

P = 128
D = 1024
T = 512
NT = T // P
ND = D // P
DEPTH = 2
HR, DKR = 4, 64
LRU_BLOCKS = 4
CONV = 4
HG = 8
NE, NG, EPG = 16, 4, 4
FE = 512
NF = FE // P
PADC = T + CONV
MAXB = (2 * T + NE * (P - 1)) // P
MINB = 2 * T // P
ALPHA = float((2.0 * DEPTH) ** 0.25)
LN_EPS, RMS_EPS = 1e-5, 1e-6
GELU_C = 2.0 * float(np.sqrt(2.0 / np.pi))
BIG = 65536.0
LEVELS = 7
R_CW, R_CB, R_GB, R_LAM, R_LB, R_NW, NROWS = 0, 16, 20, 36, 44, 60, 68


def constants():
    f = np.float32
    inv = f(10000.0) ** (-np.arange(0, DKR, 2, dtype=f) / f(DKR))
    ang = np.arange(T, dtype=f)[:, None] * inv[None, :].astype(f)
    log_gamma = np.log1p(-(2.0 ** (-5.0 - np.arange(HR, dtype=np.float64))))
    u = np.arange(T + (NT - 1) * P)[None, None, :] - (NT - 1) * P - np.arange(P)[:, None, None]
    decay = np.exp(log_gamma[None, :, None] * np.abs(u)) * DKR ** -0.5
    j = np.arange(P)
    masks = np.zeros((P, LEVELS, P), np.int32)
    for level in range(LEVELS):
        s = 1 << level
        same = (j[:, None] // (2 * s)) == (j[None, :] // (2 * s))
        masks[:, level] = same & ((j[:, None] // s) != (j[None, :] // s))
    tri = np.concatenate([np.eye(P), np.ones((P, P)), j[:, None] < j[None, :]], axis=1)
    return {
        "c_rot": np.stack([np.cos(ang), np.sin(ang)], 1).astype(f),
        "c_decay": decay.astype(f),
        "c_masks": masks,
        "c_sq": tri.astype(f),
        "c_iota": np.tile(np.arange(MAXB + 1, dtype=f)[None, :], (P, 1)),
    }


def encoder_kernel(nc, x, w_in_even, w_out_even, lru_conv_w, lru_conv_b, lru_gate_w, lru_gate_b,
                   lru_lambda, w_in_odd, w_out_odd, hg_lower_bounds, hg_norm_w, ln_w, ln_b,
                   router_w, moe_w_gate, moe_w_up, moe_w_down,
                   c_rot, c_decay, c_masks, c_sq, c_iota, out):
    with ExitStack() as ctx:
        def sb(name, shape, dt=F32):
            return ctx.enter_context(nc.sbuf_tensor(name, shape, dt))

        def sem(name):
            return ctx.enter_context(nc.semaphore(name))

        h = sb("h", [P, NT, D])
        hT = sb("hT", [P, ND, T])
        W = sb("W", [P, 24576])
        S = sb("S", [P, 18432])
        sq = sb("sq", [P, 3, P])
        rw = sb("rw", [P, ND, NE])
        prm = sb("prm", [P, NROWS])
        rot = sb("rot", [P, NT, 2, DKR // 2])
        iota = sb("iota", [P, MAXB + 1])
        sm = sb("sm", [P, 512])
        dst = sb("dst", [P, NT, 2], U32)
        gts = sb("gts", [P, NT, 2])
        tbl = sb("tbl", [1, 32], I32)
        ident, ones, upper = sq[:, 0, :], sq[:, 1, :], sq[:, 2, :]
        ps = ctx.enter_context(nc.psum_tensor("ps", [P, 8, 512], F32))

        def S3(a, n, m):
            return S[:, a:a + n * m].rearrange("p (n m) -> p n m", n=n)

        def W3(a, n, m):
            return W[:, a:a + n * m].rearrange("p (n m) -> p n m", n=n)

        def view(base, start, dims):
            return bass.AP(base.tensor, base.offset + start, [list(base.ap[0])] + dims)

        names = {}
        for name, width in (("lam", 8), ("c", 8), ("negc", 8), ("w", 8), ("w2", 8), ("p", 8), ("lbm", 8),
                            ("lbe", 16), ("lb", 8), ("olb", 8), ("rms", 4), ("rvar", 16), ("rag", 32),
                            ("rst", 96), ("st", 12), ("ag", 8), ("std", 4), ("rst1", 4)):
            names[name] = (sum(w for _, w in names.values()), width)

        def col(name, first=0, n=None):
            a, width = names[name]
            return sm[:, a + first:a + (width if n is None else first + n)]

        qk, v0, g0 = S3(0, NT, 512), S3(2048, NT, 512), S3(4096, NT, 512)
        xrp, gr = S3(6144, NT, PADC), S3(8208, NT, 512)
        qkT, ret = S3(10256, NT, 512), S3(15888, NT, 512)
        decay = S3(12304, HR, 896)
        prob = S3(0, NT, 512)
        gelu_tmp = S3(15888, NT, 512)
        W_GROUPS = [0, 1536, 512, 2048, 1024]
        w_grp = [W3(4096 * n, ND, 512) for n in range(5)]
        zero = S[:, 17936:17936 + 256]
        gate_w = W3(22528, 16, P)
        w_out0 = W3(0, ND, D)
        R = [W3(8192, NT, 512), W3(12288, NT, 512)]
        IG = [W3(10240, NT, 512), W3(14336, NT, 512)]
        A_, TMP, xc = W3(16384, NT, 512), W3(18432, NT, 512), W3(20480, NT, 512)
        mixT = hT
        v1, OG = S3(0, NT, D), S3(4096, HG, T)
        stg = S3(8192, 8, T)
        Q2, K2 = S3(12288, 2, T), S3(13312, 2, T)
        FF, TL = S3(14336, 2, T), S[:, 15360:16384]
        qs, sg, sqt, SQ = (S[:, 16384 + 512 * n:16896 + 512 * n] for n in range(4))
        ring = [W3(4096 * n, 4, ND * P).rearrange("p f (c n) -> p f c n", c=ND) for n in range(2)]
        w_v1, w_out1 = W3(8192, ND, D), W3(16384, ND, D)
        attn = W3(8192, NT, T)
        ksum = W[:, 10240:10752]
        masks = W[:, 10752:10752 + LEVELS * P].bitcast(I32).rearrange("p (l n) -> p l n", l=LEVELS)
        vh = W3(11648, NT, P)
        km = [W[:, 12160 + 512 * n:12672 + 512 * n] for n in range(2)]
        wg = [W3(12288 * n, ND, FE) for n in range(2)]
        wu = [W3(12288 * n + 4096, ND, FE) for n in range(2)]
        wd = [W3(12288 * n + 8192, NF, D) for n in range(2)]
        xg = [S[:, 1024 * n:1024 * n + 1024] for n in range(2)]
        xgT = S3(2048, ND, P)
        sig, gs, hid = (S[:, 3072 + 512 * n:3584 + 512 * n] for n in range(3))
        hidT = S3(4608, NF, P)
        yo = [S[:, 5120 + 1024 * n:6144 + 1024 * n] for n in range(2)]
        Yg = S3(7168, NT * 2, D)
        lnw, lnb = S[:, 15360:16384], S[:, 16384:17408]
        rt = S[:, 17408:18432]
        ysc = S3(0, 2, 512)

        xs = nc.dram_tensor("slot_rows", [(MAXB + 1) * P, D], F32, kind="Internal").ap()
        tok = "(n p) d -> p n d"
        rows = "(c p) n -> p c n"

        r_at = [0]

        def r_(n):
            r_at[0] += n
            return rt[:, r_at[0] - n:r_at[0]]

        r_p, r_rk, r_sel, r_x, r_msk, r_d, r_cmp = (r_(NT * NE) for _ in range(7))
        r_t4, r_grp, r_grk, r_sum, r_cnt, r_nbk, r_end, r_tb = (
            r_(n) for n in (NT, NT * NG, NT * NG, NT * NG, NE, NE, NE, 32))
        r_blk = r_((MAXB + 1) * NE)
        diag = view(attn, 0, [[T + P, NT], [1, P]])
        neighbours = view(attn, P, [[2 * T + 2 * P, 2], [T - P, 2], [1, P]])

        def sems(name, n):
            return [sem(f"{name}_{i}") for i in range(n)]

        x_in, sq_in, prm_in, tab_in, gatew_in = (sem(n) for n in ("x_in", "sq_in", "prm_in", "tab_in", "gatew_in"))
        win_in, wout_in, lnp_in = sems("win_in", 5), sem("wout_in"), sem("lnp_in")
        zero_set, xs_zeroed, pads_set = sem("zero_set"), sem("xs_zeroed"), sem("pads_set")
        ring_in, wv_in, masks_in = sems("ring_in", 2), sem("wv_in"), sem("masks_in")
        xg_in, wg_in, wu_in, wd_in = ([sems(f"{k}_in{L}", 2) for L in range(2)] for k in ("xg", "wg", "wu", "wd"))
        prmT, prmC = sem("prm_turned"), sem("prm_copied")
        hT_ps, hT_dve, hT_act = sem("hT_in_psum"), sem("hT_even_copied"), sem("hT_odd_copied")
        proj, proj_used, g_sigm = sem("proj"), sem("proj_used"), sem("g_sigmoid")
        rotated, qkT_ps, qkT_done = sem("rotated"), sem("qkT_in_psum"), sem("qkT_copied")
        conv_done, gate_ps, gate_done = sem("conv_done"), sem("gate_in_psum"), sem("gate_done")
        score_ps, prob_done, pv_ps = sem("score_in_psum"), sem("prob_done"), sem("pv_in_psum")
        lam_abs, lam_exp, lam_c = sem("lam_abs"), sem("lam_exp"), sem("lam_c")
        lb_sub, lb_exp = sem("lb_sub"), sem("lb_exp")
        a_done, tanh_done, ratio, ratio_sqrt, scanned = (sem(n) for n in (
            "a_done", "tanh_done", "ratio", "ratio_sqrt", "scanned"))
        gelu_arg, gelu_sig, gelu_done = sem("gelu_arg"), sem("gelu_sig"), sem("gelu_done")
        lru_done, ret_var, ret_std, ret_done, retT_ps, retT_done = (sem(n) for n in (
            "lru_done", "ret_var", "ret_std", "ret_done", "retT_in_psum", "retT_done"))
        op_ps, op_used, op_added = sem("outproj"), sem("outproj_used"), sem("outproj_added")
        var_done, std_done, ln_done = sem("ln_var"), sem("ln_std"), sem("ln_done")
        logits_ps, logits_sub, logits_exp, mask_done, cum_ps, table_done = (sem(k) for k in (
            "logits_in_psum", "logits_sub", "logits_exp", "mask_done", "cum_in_psum", "table_done"))
        scattered, gathered = sem("scattered"), sem("gathered")
        xgT_ps, xgT_done, gate_mm, up_mm, sig_done, act_mul, hid_done, hidT_ps, hidT_done, down_mm, y_copied = (
            sems(k, 2) for k in ("xgT_in_psum", "xgT_done", "gate_mm", "up_mm", "sig_done", "act_mul", "hid_done",
                                 "hidT_in_psum", "hidT_done", "down_mm", "y_copied"))
        y_stored = [sems(f"y_stored{L}", 2) for L in range(2)]
        v_ps, v_done, vh_done = sem("v_in_psum"), sem("v_copied"), sem("vh_copied")
        hproj, hproj_used, staged = sem("hproj"), sem("hproj_used"), sem("staged")
        prep_in, prepped, updated = sem("prep_inputs"), sem("prepped"), sem("updated")
        gram_ps, diag_done, level_done = sem("gram_in_psum"), sem("diag_done"), sem("level_done")
        off_ps, off_done = sem("off_in_psum"), sem("off_done")
        hpv_ps, hout_done, hsq_done, sq_added, sq_zero = (sem(n) for n in (
            "hpv_in_psum", "hout_done", "hsq_done", "sq_added", "sq_zeroed"))
        keys_mixed = sem("keys_mixed")
        ssq_ps, rms_var, rms_std, rms_done = sem("ssq_in_psum"), sem("rms_var"), sem("rms_std"), sem("rms_done")
        stored = sem("out_stored")
        dve_order, pool_order = sem("dve_order"), sem("pool_order")

        block = ctx.enter_context(nc.Block())

        def mixed(buf, s, first, n):
            return view(buf, first, [[2 * s, n // (2 * s)], [T + s, 2], [1, s]])

        @block.sync
        def _(sp):
            sp.dma_start(sq[:], c_sq.rearrange("p (a n) -> p a n", a=3)).then_inc(sq_in, 16)
            sp.dma_start(h[:], x[0].rearrange(tok, p=P)).then_inc(x_in, 16)
            for n, first in enumerate(W_GROUPS):
                sp.dma_start(w_grp[n], w_in_even[0][:, first:first + 512].rearrange(rows, p=P)).then_inc(win_in[n], 16)
            sp.dma_start(gate_w, lru_gate_w[0].rearrange("z g n c d -> c (z g n) d")).then_inc(gatew_in, 16)
            sp.wait_ge(proj, 20)
            sp.dma_start(w_out0, w_out_even[0].rearrange(rows, p=P)).then_inc(wout_in, 16)

            def norm_weights(n):
                sp.dma_start(lnw, ln_w[n // 2, n % 2].partition_broadcast(P)).then_inc(lnp_in, 16)
                sp.dma_start(lnb, ln_b[n // 2, n % 2].partition_broadcast(P)).then_inc(lnp_in, 16)

            def moe_loads(L):
                wgl = moe_w_gate[L].rearrange("e (c p) n -> e p c n", p=P)
                wul = moe_w_up[L].rearrange("e (c p) n -> e p c n", p=P)
                wdl = moe_w_down[L].rearrange("e (c p) n -> e p c n", p=P)
                xsb = xs.rearrange("(b p) d -> b p d", p=P)

                def expert(src, b):
                    e = sp.value_load(tbl[0:1, bass.ds(b, 1)], min_val=0, max_val=NE - 1)
                    return [w[bass.ds(e, 1)].rearrange("o p c n -> p (o c) n") for w in src]

                sp.wait_ge(table_done, L + 1)
                nb = sp.value_load(tbl[0:1, 24:25], min_val=MINB, max_val=MAXB)
                for k in range(2):
                    for t, src, s in zip((wg, wu, wd), expert((wgl, wul, wdl), k), (wg_in, wu_in, wd_in)):
                        sp.dma_start(t[k], src).then_inc(s[L][k], 16)
                sp.wait_ge(scattered, (L + 1) * 16 * 2 * NT)
                for k in range(2):
                    sp.dma_start(xg[k], xsb[k]).then_inc(xg_in[L][k], 16)

                def load(b, k):
                    with sp.If((b - 1) < nb):
                        sp.wait_ge(xgT_ps[L], (b - 1) * 2)
                        sp.dma_start(xg[k], xsb[bass.ds(b, 1)].rearrange("o p d -> p (o d)")).then_inc(xg_in[L][k], 16)
                    with sp.If(b < nb):
                        g, u, d = expert((wgl, wul, wdl), b)
                        sp.wait_ge(gate_mm[L], b - 1)
                        sp.dma_start(wg[k], g).then_inc(wg_in[L][k], 16)
                        sp.wait_ge(up_mm[L], b - 1)
                        sp.dma_start(wu[k], u).then_inc(wu_in[L][k], 16)
                        sp.wait_ge(down_mm[L], (b - 1) * 2)
                        sp.dma_start(wd[k], d).then_inc(wd_in[L][k], 16)

                with sp.Fori(2, MAXB - 2, 2) as b:
                    for k in range(2):
                        load(b + k, k)
                with sp.Fori(MAXB - 1, MAXB, 1) as b:
                    load(b, 0)
                return nb

            sp.wait_ge(retT_ps, NT)
            sp.wait_ge(lru_done, 1)
            norm_weights(0)
            sp.wait_ge(ln_done, NT)
            norm_weights(1)
            nb0 = moe_loads(0)

            w5 = w_in_odd[0].rearrange("(c p) (f h n) -> f h p c n", p=P, f=5, h=HG)

            def head_weights(hd, slot):
                for n, f in enumerate((0, 2, 3, 4)):
                    sp.dma_start(ring[slot][:, n], w5[f, bass.ds(hd, 1)].rearrange("o p c n -> p (o c) n")
                                 ).then_inc(ring_in[slot], 16)

            sp.wait_ge(down_mm[0], nb0 * 2)
            sp.dma_start(w_v1, w_in_odd[0][:, D:2 * D].rearrange(rows, p=P)).then_inc(wv_in, 16)
            head_weights(0, 0)
            head_weights(1, 1)
            sp.dma_start(w_out1, w_out_odd[0].rearrange(rows, p=P)).then_inc(wout_in, 16)
            sp.wait_ge(v_ps, 2 * NT)
            sp.dma_start(masks, c_masks).then_inc(masks_in, 16)
            with sp.Fori(2, HG - 1, 2) as hd:
                for k in range(2):
                    sp.wait_ge(hproj, (hd + k - 1) * 4)
                    head_weights(hd + k, k)
            sp.wait_ge(hout_done, HG)
            sp.wait_ge(ln_done, 2 * NT)
            norm_weights(2)
            sp.wait_ge(ln_done, 3 * NT)
            norm_weights(3)
            moe_loads(1)
            for t in range(NT):
                sp.wait_ge(ln_done, 3 * NT + t + 1)
                sp.dma_start(out[0, t * P:(t + 1) * P, :], h[:, t, :]).then_inc(stored, 16)
            sp.wait_ge(stored, 16 * NT)

        @block.tensor
        def _(pe):
            def turn_h(n):
                for k in range(2 * NT):
                    t, half = k // 2, k % 2
                    if half == 0 and n > 0:
                        pe.wait_ge(ln_done, (n - 1) * NT + t + 1)
                    if k >= 4:
                        pe.wait_ge((hT_dve, hT_act)[k % 2], n * NT + (k - 4) // 2 + 1)
                    for c in range(4):
                        last = pe.transpose(ps[:, k % 4, c * P:(c + 1) * P],
                                            h[:, t, (half * 4 + c) * P:(half * 4 + c + 1) * P], ident)
                    last.then_inc(hT_ps, 1)
                pe.wait_ge(hT_dve, (n + 1) * NT)
                pe.wait_ge(hT_act, (n + 1) * NT)

            pe.wait_ge(sq_in, 16)
            pe.wait_ge(prm_in, 16 * 6)
            pe.transpose(ps[:, 4, 0:NROWS], S[0:NROWS, 0:P], ident[0:NROWS, 0:NROWS]).then_inc(prmT, 1)
            pe.wait_ge(x_in, 16)
            turn_h(0)
            pe.wait_ge(prmC, 1)

            def project(n):
                grp, i = n // 4, n % 4
                if i == 0:
                    pe.wait_ge(win_in[grp], 16)
                if n >= 4:
                    pe.wait_ge(proj_used, n - 3)
                for c in range(ND):
                    if grp in (1, 3):
                        a, b = w_grp[grp][:, c, i * P:(i + 1) * P], hT[:, c, :]
                    else:
                        a, b = hT[:, c, i * P:(i + 1) * P], w_grp[grp][:, c, :]
                    last = pe.matmul(ps[:, 4 + n % 4, :], a, b, start=(c == 0), stop=(c == ND - 1))
                last.then_inc(proj, 1)

            for n in range(12):
                project(n)
            for t in range(NT):
                pe.wait_ge(rotated, t + 1)
                for c in range(4):
                    last = pe.transpose(ps[:, t, c * P:(c + 1) * P], qk[:, t, c * P:(c + 1) * P], ident)
                last.then_inc(qkT_ps, 1)
            for n in range(12, 20):
                project(n)
            pe.wait_ge(qkT_done, NT)
            pe.wait_ge(gatew_in, 16)
            pe.wait_ge(conv_done, NT)
            for k in range(16):
                n, zg = k // 4, k % 4
                if k >= 4:
                    pe.wait_ge(gate_done, k - 3)
                pe.matmul(ps[:, k % 4, :], gate_w[:, zg * 4 + n, :], xc[:, n, :], start=True, stop=True
                          ).then_inc(gate_ps, 1)
            pe.wait_ge(proj_used, 20)
            for hd in range(HR):
                lo = DKR * (hd % 2)
                for j in range(NT):
                    if hd == 0:
                        pe.wait_ge(gate_done, 13 + j)
                    else:
                        pe.wait_ge(prob_done, (hd - 1) * NT + j + 1)
                    pe.matmul(ps[:, j, :], qkT[lo:lo + DKR, 2 + hd // 2, j * P:(j + 1) * P],
                              qkT[lo:lo + DKR, hd // 2, :], start=True, stop=True).then_inc(score_ps, 1)
                pe.wait_ge(prob_done, (hd + 1) * NT)
                for t in range(NT):
                    for j in range(NT):
                        last = pe.matmul(ps[:, 4 + t, hd * P:(hd + 1) * P], prob[:, j, t * P:(t + 1) * P],
                                         v0[:, j, hd * P:(hd + 1) * P], start=(j == 0), stop=(j == NT - 1))
                last.then_inc(pv_ps, 1)
            for t in range(NT):
                pe.wait_ge(ret_done, t + 1)
                for c in range(4):
                    last = pe.transpose(ps[:, t, c * P:(c + 1) * P], ret[:, t, c * P:(c + 1) * P], ident)
                last.then_inc(retT_ps, 1)
            pe.wait_ge(retT_done, NT)
            pe.wait_ge(lru_done, 1)

            def out_project(L, srcT, w):
                pe.wait_ge(wout_in, 16 * (L + 1))
                for k in range(2 * NT):
                    t, half = k // 2, k % 2
                    if k >= 4:
                        pe.wait_ge(op_used, L * 2 * NT + k - 3)
                    for c in range(ND):
                        last = pe.matmul(ps[:, 4 + k % 4, :], srcT[:, c, t * P:(t + 1) * P],
                                         w[:, c, half * 512:(half + 1) * 512], start=(c == 0), stop=(c == ND - 1))
                    last.then_inc(op_ps, 1)

            def router(L):
                pe.wait_ge(op_used, (L + 1) * 2 * NT)
                for t in range(NT):
                    for c in range(ND):
                        last = pe.matmul(ps[:, 4, t * NE:(t + 1) * NE], hT[:, c, t * P:(t + 1) * P], rw[:, c, :],
                                         start=(c == 0), stop=(c == ND - 1))
                last.then_inc(logits_ps, 1)
                pe.wait_ge(mask_done, L + 1)
                for t in range(NT):
                    for u in range(t + 1):
                        pe.matmul(ps[:, 5, t * NE:(t + 1) * NE], upper if u == t else ones,
                                  r_msk[:, u * NE:(u + 1) * NE], start=(u == 0), stop=(u == t))
                for u in range(NT):
                    last = pe.matmul(ps[:, 5, 64:64 + NE], ones, r_msk[:, u * NE:(u + 1) * NE],
                                     start=(u == 0), stop=(u == NT - 1))
                last.then_inc(cum_ps, 1)

            def moe(L):
                pe.wait_ge(table_done, L + 1)
                nb = pe.value_load(tbl[0:1, 24:25], min_val=MINB, max_val=MAXB)

                def turn_rows(b, k, loads):
                    pe.wait_ge(xg_in[L][k], loads)
                    for half in range(2):
                        for c in range(4):
                            last = pe.transpose(ps[:, 4 + half, c * P:(c + 1) * P],
                                                xg[k][:, (half * 4 + c) * P:(half * 4 + c + 1) * P], ident)
                        last.then_inc(xgT_ps[L], 1)

                def gate_up(b, k, loads):
                    pe.wait_ge(xgT_done[L], (b + 1) * 2)
                    for bank, w, w_in, done in ((0, wg, wg_in, gate_mm), (1, wu, wu_in, up_mm)):
                        pe.wait_ge(w_in[L][k], loads)
                        for c in range(ND):
                            last = pe.matmul(ps[:, bank, :], xgT[:, c, :], w[k][:, c, :],
                                             start=(c == 0), stop=(c == ND - 1))
                        last.then_inc(done[L], 1)

                def turn_hidden(b):
                    pe.wait_ge(hid_done[L], b + 1)
                    for c in range(NF):
                        last = pe.transpose(ps[:, 6, c * P:(c + 1) * P], hid[:, c * P:(c + 1) * P], ident)
                    last.then_inc(hidT_ps[L], 1)

                def down(b, k, loads, first=False):
                    pe.wait_ge(wd_in[L][k], loads)
                    pe.wait_ge(hidT_done[L], b + 1)
                    if not first:
                        pe.wait_ge(y_copied[L], b * 2)
                    for half in range(2):
                        for c in range(NF):
                            last = pe.matmul(ps[:, 2 + half, :], hidT[:, c, :],
                                             wd[k][:, c, half * 512:(half + 1) * 512],
                                             start=(c == 0), stop=(c == NF - 1))
                        last.then_inc(down_mm[L], 1)

                turn_rows(0, 0, 16)
                gate_up(0, 0, 16)
                turn_rows(1, 1, 16)
                turn_hidden(0)
                gate_up(1, 1, 16)
                down(0, 0, 16, first=True)
                turn_rows(2, 0, 32)
                turn_hidden(1)
                with pe.Fori(2, MAXB - 2, 2) as b:
                    for k in range(2):
                        with pe.If((b + k) < nb):
                            gate_up(b + k, k, (b + 2) * 8)
                            down(b + k - 1, 1 - k, (b + 2 * k) * 8)
                            turn_rows(b + k + 1, 1 - k, (b + 2 + 2 * k) * 8)
                            turn_hidden(b + k)
                        with pe.If((b + k) == nb):
                            down(b + k - 1, 1 - k, (b + 2 * k) * 8)
                last_b = MAXB - 1
                with pe.Fori(last_b, MAXB, 1) as b:
                    with pe.If(b < nb):
                        gate_up(b, 0, (b + 2) * 8)
                        down(b - 1, 1, b * 8)
                        turn_hidden(b)
                        down(b, 0, (b + 2) * 8)
                    with pe.If(b == nb):
                        down(b - 1, 1, b * 8)

            out_project(0, mixT, w_out0)
            turn_h(1)
            router(0)
            moe(0)
            turn_h(2)

            pe.wait_ge(wv_in, 16)
            for k in range(2 * NT):
                t, half = k // 2, k % 2
                if k >= 2:
                    pe.wait_ge(v_done, k - 1)
                for c in range(ND):
                    last = pe.matmul(ps[:, k % 2, :], hT[:, c, t * P:(t + 1) * P],
                                     w_v1[:, c, half * 512:(half + 1) * 512], start=(c == 0), stop=(c == ND - 1))
                last.then_inc(v_ps, 1)
            pe.wait_ge(v_done, 2 * NT)

            def head_project(hd, slot, f, tiles, first=False):
                if tiles[0] == 0:
                    if f == 0:
                        pe.wait_ge(ring_in[slot], (hd - slot + 2) * 32)
                    if not first or f >= 2:
                        pe.wait_ge(hproj_used, hd * 4 + f - 1)
                for c in tiles:
                    last = pe.matmul(ps[:, f % 2, :], ring[slot][:, f, c, :], hT[:, c, :],
                                     start=(c == 0), stop=(c == ND - 1))
                if tiles[-1] == ND - 1:
                    last.then_inc(hproj, 1)

            def gram(hd, level):
                if level == 0:
                    pe.wait_ge(prepped, hd + 1)
                if level == 2:
                    pe.wait_ge(diag_done, hd + 1)
                if level >= 1:
                    pe.wait_ge(keys_mixed, hd * LEVELS + level)
                if level >= 3:
                    pe.wait_ge(level_done, hd * LEVELS + level - 2)
                for c in range(NT):
                    o = ps[:, 2 + level % 2, c * P:(c + 1) * P]
                    if level == 0:
                        last = pe.matmul(o, ksum[:, c * P:(c + 1) * P], qs[:, c * P:(c + 1) * P], start=True, stop=True)
                    else:
                        s = 1 << (level - 1)
                        last = pe.matmul(o, km[level % 2][:, c * P:(c + 1) * P], mixed(Q2, s, c * P, P), start=True, stop=True)
                last.then_inc(gram_ps, 1)

            def gram_off(hd):
                pe.wait_ge(updated, hd * 8 + 7)
                for j in range(NT):
                    i = j ^ 1
                    last = pe.matmul(ps[:, 4, j * P:(j + 1) * P], K2[:, j % 2, j * P:(j + 1) * P],
                                     Q2[:, i % 2, i * P:(i + 1) * P], start=True, stop=True)
                last.then_inc(off_ps, 1)

            def gram_pairs(hd):
                pe.wait_ge(updated, hd * 8 + 8)
                for j in range(NT):
                    i = 1 - j // 2
                    last = pe.matmul(ps[:, 5 + j // 2, (j % 2) * 256:(j % 2 + 1) * 256],
                                     K2[:, j // 2, j * P:(j + 1) * P],
                                     Q2[:, i, i * 256:(i + 1) * 256], start=True, stop=True)
                last.then_inc(off_ps, 1)

            def head_pv(hd, first=False):
                pe.wait_ge(level_done, hd * LEVELS + LEVELS)
                pe.wait_ge(off_done, hd * 2 + 2)
                pe.wait_ge(vh_done, hd + 1)
                if not first:
                    pe.wait_ge(hsq_done, hd)
                for j in range(NT):
                    last = pe.matmul(ps[:, 7, :], vh[:, j, :], attn[:, j, :], start=(j == 0), stop=(j == NT - 1))
                last.then_inc(hpv_ps, 1)

            def attend(hd, slot, first=False):
                parts = [(f, range(a, a + 4)) for f in range(4) for a in (0, 4)] if slot is not None else []

                def fill(n=1):
                    for _ in range(n):
                        if parts:
                            f, tiles = parts.pop(0)
                            head_project(hd + 1, slot, f, tiles)

                fill(2)
                for level in range(LEVELS + 1):
                    gram(hd, level)
                    if level in (1, 2, 3, 4, 5):
                        fill()
                gram_off(hd)
                fill()
                gram_pairs(hd)
                fill(9)
                head_pv(hd, first)

            for f in range(4):
                head_project(0, 0, f, range(ND), first=True)
            attend(0, 1, first=True)
            attend(1, 0)
            with pe.Fori(2, HG - 3, 2) as hd:
                attend(hd, 1)
                attend(hd + 1, 0)
            attend(HG - 2, 1)
            attend(HG - 1, None)
            pe.wait_ge(sq_added, HG)
            for t in range(NT):
                last = pe.matmul(ps[:, 0, t:t + 1], SQ[:, t * P:(t + 1) * P], ones[:, 0:1], start=True, stop=True)
            last.then_inc(ssq_ps, 1)
            pe.wait_ge(hout_done, HG)
            pe.wait_ge(hsq_done, HG)
            out_project(1, OG, w_out1)
            turn_h(3)
            router(1)
            moe(1)

        @block.scalar
        def _(act):
            def copy(o, i):
                return nc.scalar.activation(o, i, ACT.Copy)

            def turn_copies(n):
                for k in range(1, 2 * NT, 2):
                    act.wait_ge(hT_ps, n * 2 * NT + k + 1)
                    copy(hT[:, 4:8, (k // 2) * P:(k // 2 + 1) * P],
                         ps[:, k % 4, :].rearrange("p (c n) -> p c n", c=4)).then_inc(hT_act, 1)

            for first, a, n in ((R_CW, lru_conv_w[0].rearrange("j (b c) -> (j b) c", c=P), 16),
                                (R_CB, lru_conv_b[0].rearrange("(b c) -> b c", c=P), 4),
                                (R_GB, lru_gate_b[0].rearrange("z g n c -> (z g n) c"), 16),
                                (R_LAM, lru_lambda[0].rearrange("z (b c) -> (z b) c", c=P), 8),
                                (R_LB, hg_lower_bounds.rearrange("l (b c) -> (l b) c", c=P), 16),
                                (R_NW, hg_norm_w[0].rearrange("(b c) -> b c", c=P), 8)):
                act.dma_start(S[first:first + n, 0:P], a).then_inc(prm_in, 16)
            act.dma_start(rot[:], c_rot.rearrange("(n p) a k -> p n a k", p=P)).then_inc(tab_in, 16)
            act.dma_start(rw[:], router_w.rearrange(rows, p=P)).then_inc(tab_in, 16)
            act.dma_start(iota[:], c_iota).then_inc(tab_in, 16)
            act.dma_start(decay, c_decay).then_inc(tab_in, 16)
            act.wait_ge(prmT, 1)
            copy(prm[:], ps[:, 4, 0:NROWS]).then_inc(prmC, 1)
            turn_copies(0)
            act.wait_ge(lam_abs, 1)
            nc.scalar.activation(col("lam"), col("lam"), ACT.Exp, scale=-1.0).then_inc(lam_exp, 1)
            act.wait_ge(lb_sub, 1)
            nc.scalar.activation(col("lbe"), col("lbe"), ACT.Exp).then_inc(lb_exp, 1)
            act.wait_ge(zero_set, 1)
            act.wait_ge(win_in[1], 16)
            zrows = xs.rearrange("(p b) (q e) -> p (b q) e", p=P, e=256)
            for n in range(0, (MAXB + 1) * 4, 24):
                act.dma_start(zrows[:, n:n + 24, :], view(zero, 0, [[0, 24], [1, 256]])).then_inc(xs_zeroed, 16)
            act.wait_ge(pads_set, 1)
            for n in range(20):
                grp, i = n // 4, n % 4
                act.wait_ge(proj, n + 1)
                bank = ps[:, 4 + n % 4, :]
                if grp == 4:
                    nc.scalar.activation(g0[:, i, :], bank, ACT.Sigmoid).then_inc(g_sigm, 1)
                else:
                    to = {0: qk[:, i, :], 1: xrp[:, i, 2:2 + T], 2: v0[:, i, :], 3: gr[:, i, :]}[grp]
                    copy(to, bank).then_inc(proj_used, 1)
            for k in range(16):
                n, zg = k // 4, k % 4
                act.wait_ge(gate_ps, k + 1)
                nc.scalar.activation((R, IG)[zg % 2][zg // 2][:, n, :], ps[:, k % 4, :], ACT.Sigmoid,
                                     bias=prm[:, R_GB + zg * 4 + n:R_GB + zg * 4 + n + 1]).then_inc(gate_done, 1)
            act.wait_ge(gelu_arg, 1)
            nc.scalar.activation(gelu_tmp, gelu_tmp, ACT.Sigmoid, scale=GELU_C).then_inc(gelu_sig, 1)
            act.wait_ge(lam_c, 1)
            act.wait_ge(gate_done, 16)
            for z in range(2):
                if z == 1:
                    act.wait_ge(ret_var, 1)
                    nc.scalar.activation(col("rvar"), col("rvar"), ACT.Sqrt).then_inc(ret_std, 1)
                    act.wait_ge(scanned, 1)
                for n in range(NT):
                    last = nc.scalar.activation(A_[:, n, :], R[z][:, n, :], ACT.Exp, scale=col("negc", z * 4 + n, 1))
                last.then_inc(a_done, 1)
                act.wait_ge(a_done, z + 1)
                for n in range(NT):
                    last = nc.scalar.activation(R[z][:, n, :], R[z][:, n, :], ACT.Tanh, scale=col("c", z * 4 + n, 1))
                last.then_inc(tanh_done, 1)
                act.wait_ge(ratio, z + 1)
                nc.scalar.activation(TMP, TMP, ACT.Sqrt).then_inc(ratio_sqrt, 1)

            def norm_std(n, tiles=range(NT)):
                for t in tiles:
                    act.wait_ge(var_done, n * NT + t + 1)
                    nc.scalar.activation(col("std", t, 1), col("std", t, 1), ACT.Sqrt).then_inc(std_done, 1)

            def moe(L):
                act.wait_ge(logits_sub, L + 1)
                nc.scalar.activation(r_p, r_p, ACT.Exp).then_inc(logits_exp, 1)
                act.wait_ge(table_done, L + 1)
                nb = act.value_load(tbl[0:1, 24:25], min_val=MINB, max_val=MAXB)
                ysb = xs.rearrange("(b p) d -> b p d", p=P)

                def sigmoid(b, first=False):
                    act.wait_ge(gate_mm[L], b + 1)
                    if not first:
                        act.wait_ge(act_mul[L], b)
                    nc.scalar.activation(sig, ps[:, 0, :], ACT.Sigmoid).then_inc(sig_done[L], 1)

                def store(b, k, early=False):
                    if not early:
                        act.wait_ge(y_stored[L][k], (b - k) * 8)
                    for half in range(2):
                        act.wait_ge(down_mm[L], b * 2 + half + 1)
                        copy(yo[k][:, half * 512:(half + 1) * 512], ps[:, 2 + half, :]).then_inc(y_copied[L], 1)
                    act.wait_ge(y_copied[L], b * 2 + 2)
                    act.dma_start(ysb[bass.ds(b, 1)].rearrange("o p d -> p (o d)"), yo[k]).then_inc(y_stored[L][k], 16)

                sigmoid(0, first=True)
                sigmoid(1)
                store(0, 0, early=True)
                sigmoid(2)
                store(1, 1, early=True)
                with act.Fori(3, MAXB - 1, 2) as b:
                    for k in range(2):
                        with act.If((b + k) < nb):
                            sigmoid(b + k)
                            store(b + k - 1, k)
                        with act.If((b + k) == nb):
                            store(b + k - 1, k)

            norm_std(0)
            turn_copies(1)
            moe(0)
            norm_std(1)
            turn_copies(2)
            for k in range(2 * NT):
                act.wait_ge(v_ps, k + 1)
                copy(v1[:, k // 2, (k % 2) * 512:(k % 2 + 1) * 512], ps[:, k % 2, :]).then_inc(v_done, 1)

            def stage(hd, f, first=False):
                act.wait_ge(hproj, hd * 4 + f + 1)
                if not first and f == 0:
                    act.wait_ge(prepped, hd)
                bank = ps[:, f % 2, :]
                if f in (0, 3):
                    a = {0: 0, 3: 2}[f]
                    copy(stg[:, a, :], bank)
                    nc.scalar.activation(stg[:, a + 1, :], bank, ACT.Sigmoid).then_inc(hproj_used, 1)
                else:
                    pos, neg = {1: (5, 6), 2: (4, 7)}[f]
                    nc.scalar.activation(stg[:, pos, :], bank, ACT.Sigmoid)
                    nc.scalar.activation(stg[:, neg, :], bank, ACT.Sigmoid, scale=-1.0).then_inc(hproj_used, 1)

            def scores(hd, last, first=False):
                if not first:
                    act.wait_ge(hpv_ps, hd)
                act.wait_ge(gram_ps, hd * 8 + 1)
                if first:
                    act.wait_ge(masks_in, 16)
                copy(diag, ps[:, 2, :].rearrange("p (c n) -> p c n", c=NT)).then_inc(diag_done, 1)
                if not last:
                    for f in range(2):
                        stage(hd + 1, f)
                    stage(hd + 1, 2)
                act.wait_ge(off_ps, hd * 2 + 1)
                copy(neighbours, ps[:, 4, :].rearrange("p (a b n) -> p a b n", a=2, b=2)).then_inc(off_done, 1)
                act.wait_ge(off_ps, hd * 2 + 2)
                copy(attn[:, 0:2, 256:512], ps[:, 5, :].rearrange("p (a n) -> p a n", a=2))
                copy(attn[:, 2:4, 0:256], ps[:, 6, :].rearrange("p (a n) -> p a n", a=2)).then_inc(off_done, 1)
                if not last:
                    stage(hd + 1, 3)
                if not first:
                    act.wait_ge(sq_added, hd)
                act.wait_ge(hout_done, hd + 1)
                nc.scalar.activation(sqt, ps[:, 7, :], ACT.Square).then_inc(hsq_done, 1)

            for f in range(4):
                stage(0, f, first=True)
            scores(0, False, first=True)
            with act.Fori(1, HG - 1, 1) as hd:
                scores(hd, False)
            scores(HG - 1, True)
            act.wait_ge(rms_var, 1)
            nc.scalar.activation(col("rms"), col("rms"), ACT.Sqrt).then_inc(rms_std, 1)
            act.wait_ge(rms_done, 1)
            for t in range(NT):
                for k in (2 * t, 2 * t + 1):
                    act.wait_ge(op_ps, 2 * NT + k + 1)
                    if k >= 2:
                        act.wait_ge(op_added, k - 1)
                    nc.scalar.activation(ysc[:, k % 2, :], ps[:, 4 + k % 4, :], ACT.Copy,
                                         scale=col("rms", t, 1)).then_inc(op_used, 1)
                if t > 0:
                    norm_std(2, [t - 1])
            norm_std(2, [NT - 1])
            turn_copies(3)
            moe(1)
            norm_std(3)

        @block.vector
        def _(dve):
            v = nc.vector
            count = [0]

            def done(ins):
                count[0] += 1
                ins.then_inc(dve_order, 1)
                dve.wait_ge(dve_order, count[0])

            def turn_copies(n):
                for k in range(0, 2 * NT, 2):
                    dve.wait_ge(hT_ps, n * 2 * NT + k + 1)
                    v.tensor_copy(hT[:, 0:4, (k // 2) * P:(k // 2 + 1) * P],
                                  ps[:, k % 4, :].rearrange("p (c n) -> p c n", c=4)).then_inc(hT_dve, 1)

            dve.wait_ge(prmC, 1)
            lam = prm[:, R_LAM:R_LAM + 8]
            v.scalar_tensor_tensor(col("lam"), lam, -1.0, lam, ALU.mult, ALU.max).then_inc(lam_abs, 1)
            lb0, lb1 = prm[:, R_LB:R_LB + 8], prm[:, R_LB + 8:R_LB + 16]
            done(v.tensor_tensor(col("lbm"), lb0, lb1, ALU.max))
            v.tensor_tensor(col("lbe", 0, 8), lb0, col("lbm"), ALU.subtract)
            v.tensor_tensor(col("lbe", 8, 8), lb1, col("lbm"), ALU.subtract).then_inc(lb_sub, 1)
            turn_copies(0)
            dve.wait_ge(lam_exp, 1)
            done(v.tensor_scalar(col("w"), col("lam"), 2.0, None, ALU.add))
            done(v.reciprocal(col("w"), col("w")))
            done(v.tensor_tensor(col("w"), col("w"), col("lam"), ALU.mult))
            done(v.tensor_tensor(col("w2"), col("w"), col("w"), ALU.mult))
            done(v.tensor_scalar(col("p"), col("w2"), 1.0 / 15, None, ALU.mult))
            for n in (13, 11, 9, 7, 5, 3):
                done(v.scalar_tensor_tensor(col("p"), col("p"), 1.0 / n, col("w2"), ALU.add, ALU.mult))
            done(v.scalar_tensor_tensor(col("p"), col("p"), 1.0, col("w"), ALU.add, ALU.mult))
            done(v.tensor_scalar(col("w2"), lam, -1.0, 0.0, ALU.mult, ALU.max))
            done(v.scalar_tensor_tensor(col("p"), col("p"), 2.0, col("w2"), ALU.mult, ALU.add))
            v.tensor_scalar(col("negc"), col("p"), -8.0, None, ALU.mult)
            v.tensor_scalar(col("c"), col("p"), 8.0, None, ALU.mult).then_inc(lam_c, 1)
            dve.wait_ge(lb_exp, 1)
            done(v.tensor_tensor(col("lbm"), col("lbe", 0, 8), col("lbe", 8, 8), ALU.add))
            done(v.reciprocal(col("lbm"), col("lbm")))
            done(v.tensor_tensor(col("lb"), col("lbe", 8, 8), col("lbm"), ALU.mult))
            done(v.tensor_scalar(col("olb"), col("lb"), -1.0, 1.0, ALU.mult, ALU.add))

            dve.wait_ge(tab_in, 64)
            pairs = [[DKR, 2 * HR], [2, DKR // 2]]
            tmp = [view(gelu_tmp, 256 * n, [[DKR // 2, 2 * HR], [1, DKR // 2]]) for n in range(4)]
            for t in range(NT):
                dve.wait_ge(proj_used, t + 1)
                if t > 0:
                    dve.wait_ge(rotated, t)
                x1, x2 = view(qk, t * 512, pairs), view(qk, t * 512 + 1, pairs)
                cos, sin = (view(rot[:], (2 * t + n) * (DKR // 2), [[0, 2 * HR], [1, DKR // 2]]) for n in range(2))
                v.tensor_tensor(tmp[0], x1, cos, ALU.mult)
                v.tensor_tensor(tmp[1], x2, sin, ALU.mult)
                v.tensor_tensor(tmp[2], x1, sin, ALU.mult)
                done(v.tensor_tensor(tmp[3], x2, cos, ALU.mult))
                v.tensor_tensor(x1, tmp[0], tmp[1], ALU.subtract)
                v.tensor_tensor(x2, tmp[2], tmp[3], ALU.add).then_inc(rotated, 1)
            for n in range(LRU_BLOCKS):
                dve.wait_ge(proj_used, 5 + n)

                def tap(j):
                    return prm[:, R_CW + 4 * j + n:R_CW + 4 * j + n + 1]

                done(v.tensor_scalar(xc[:, n, :], xrp[:, n, 0:T], tap(0), prm[:, R_CB + n:R_CB + n + 1],
                                     ALU.mult, ALU.add))
                for j in (1, 2, 3):
                    ins = v.scalar_tensor_tensor(xc[:, n, :], xrp[:, n, j:j + T], tap(j), xc[:, n, :], ALU.mult, ALU.add)
                    if j < 3:
                        done(ins)
                ins.then_inc(conv_done, 1)
            for t in range(NT):
                dve.wait_ge(qkT_ps, t + 1)
                v.tensor_copy(qkT[:, :, t * P:(t + 1) * P], ps[:, t, :].rearrange("p (c n) -> p c n", c=4)
                              ).then_inc(qkT_done, 1)
            for i in range(NT):
                dve.wait_ge(g_sigm, i + 1)
                v.tensor_tensor(g0[:, i, :], g0[:, i, :], ps[:, 4 + i, :], ALU.mult).then_inc(proj_used, 1)
            for hd in range(HR):
                for j in range(NT):
                    dve.wait_ge(score_ps, hd * NT + j + 1)
                    if hd > 0:
                        dve.wait_ge(pv_ps, hd)
                    at = (NT - 1 - j) * P
                    v.tensor_tensor(prob[:, j, :], ps[:, j, :], decay[:, hd, at:at + T], ALU.mult).then_inc(prob_done, 1)

            def gate_ratio(z):
                dve.wait_ge(gate_done, 16)
                v.tensor_tensor(IG[z], IG[z], xc, ALU.mult)
                dve.wait_ge(tanh_done, z + 1)
                done(v.tensor_scalar(TMP, R[z], 1.0, None, ALU.add))
                done(v.reciprocal(TMP, TMP))
                v.scalar_tensor_tensor(TMP, TMP, 2.0, R[z], ALU.mult, ALU.mult).then_inc(ratio, 1)

            def scan(z):
                dve.wait_ge(ratio_sqrt, z + 1)
                dve.wait_ge(ratio, z + 1)
                done(v.tensor_tensor(IG[z], IG[z], TMP, ALU.mult))
                for n in range(LRU_BLOCKS):
                    if z == 0:
                        o, a, b = R[0][:, n, :], A_[:, n, :], IG[0][:, n, :]
                    else:
                        o, a, b = (view(buf, n * T + T - 1, [[-1, T]]) for buf in (R[1], A_, IG[1]))
                    ins = v.tensor_tensor_scan(o, a, b, 0.0, ALU.mult, ALU.add)
                ins.then_inc(scanned, 1)

            gate_ratio(0)
            dve.wait_ge(pv_ps, HR)
            for t in range(NT):
                for hd in range(HR):
                    last = v.bn_stats(col("rst", 6 * (t * HR + hd), 6), ps[:, 4 + t, hd * P:(hd + 1) * P])
            done(last)
            for n in range(NT * HR):
                last = v.bn_aggr(col("rag", 2 * n, 2), col("rst", 6 * n, 6))
            done(last)
            v.tensor_scalar(col("rvar"), view(col("rag"), 1, [[2, NT * HR]]), LN_EPS, None, ALU.add).then_inc(ret_var, 1)
            scan(0)
            dve.wait_ge(ret_std, 1)
            done(v.reciprocal(col("rvar"), col("rvar")))
            dve.wait_ge(gelu_done, 1)
            for t in range(NT):
                for hd in range(HR):
                    n = t * HR + hd
                    last = v.tensor_scalar(ret[:, t, hd * P:(hd + 1) * P], ps[:, 4 + t, hd * P:(hd + 1) * P],
                                           col("rag", 2 * n, 1), col("rvar", n, 1), ALU.subtract, ALU.mult)
                done(last)
                v.tensor_tensor(ret[:, t, :], ret[:, t, :], g0[:, t, :], ALU.mult).then_inc(ret_done, 1)
            gate_ratio(1)
            for t in range(NT):
                dve.wait_ge(retT_ps, t + 1)
                v.tensor_copy(mixT[:, 0:4, t * P:(t + 1) * P], ps[:, t, :].rearrange("p (c n) -> p c n", c=4)
                              ).then_inc(retT_done, 1)
            scan(1)
            dve.wait_ge(scanned, 2)
            done(v.tensor_tensor(R[0], R[0], R[1], ALU.add))
            v.tensor_tensor(mixT[:, 4:8, :], R[0], gr, ALU.mult).then_inc(lru_done, 1)

            def norm_stats(n, t):
                for half in range(2):
                    last = v.bn_stats(col("st", 6 * half, 6), h[:, t, half * 512:(half + 1) * 512])
                done(last)
                done(v.bn_aggr(col("ag", 2 * t, 2), col("st")))
                v.tensor_scalar(col("std", t, 1), col("ag", 2 * t + 1, 1), LN_EPS, None, ALU.add).then_inc(var_done, 1)

            def norm_apply(n, t):
                dve.wait_ge(std_done, n * NT + t + 1)
                done(v.reciprocal(col("rst1", t, 1), col("std", t, 1)))
                done(v.tensor_scalar(h[:, t, :], h[:, t, :], col("ag", 2 * t, 1), col("rst1", t, 1),
                                     ALU.subtract, ALU.mult))
                if t == 0:
                    dve.wait_ge(lnp_in, 32 * (n + 1))
                done(v.tensor_tensor(h[:, t, :], h[:, t, :], lnw, ALU.mult))
                v.tensor_tensor(h[:, t, :], h[:, t, :], lnb, ALU.add).then_inc(ln_done, 1)

            def norm(n, add):
                for t in range(NT + 1):
                    if t < NT:
                        add(t)
                        norm_stats(n, t)
                    if t > 0:
                        norm_apply(n, t - 1)

            def add_mixer(L):
                def add(t):
                    for half in range(2):
                        k = 2 * t + half
                        hh = h[:, t, half * 512:(half + 1) * 512]
                        if L == 0:
                            dve.wait_ge(op_ps, k + 1)
                            v.scalar_tensor_tensor(hh, hh, ALPHA, ps[:, 4 + k % 4, :], ALU.mult, ALU.add
                                                   ).then_inc(op_used, 1)
                        else:
                            dve.wait_ge(op_used, 2 * NT + k + 1)
                            v.scalar_tensor_tensor(hh, hh, ALPHA, ysc[:, k % 2, :], ALU.mult, ALU.add
                                                   ).then_inc(op_added, 1)
                    dve.wait_ge((op_used, op_added)[L], 2 * t + 2)
                return add

            def add_moe(L):
                def add(t):
                    if t == 0:
                        dve.wait_ge(gathered, (L + 1) * 16 * 2 * NT)
                    done(v.tensor_scalar(h[:, t, :], h[:, t, :], ALPHA, None, ALU.mult))
                    for k in range(2):
                        done(v.scalar_tensor_tensor(h[:, t, :], Yg[:, 2 * t + k, :], gts[:, t, k:k + 1], h[:, t, :],
                                                    ALU.mult, ALU.add))
                return add

            def rank(rk, val, n):
                done(v.memset(rk, 0.0))
                for a in range(EPG - 1):
                    m = EPG - 1 - a
                    cmp_ = view(r_cmp, 0, [[m, n], [1, m]])
                    done(v.tensor_tensor(cmp_, view(val, a, [[EPG, n], [0, m]]), view(val, a + 1, [[EPG, n], [1, m]]),
                                         ALU.is_ge))
                    later = view(rk, a + 1, [[EPG, n], [1, m]])
                    here = view(rk, a, [[EPG, n]])
                    v.tensor_tensor(later, later, cmp_, ALU.add)
                    done(v.tensor_reduce(view(r_sum, 0, [[1, n]]), cmp_, AX.X, ALU.add))
                    done(v.scalar_tensor_tensor(here, here, float(m), view(r_sum, 0, [[1, n]]), ALU.add, ALU.subtract))

            def route(L):
                def by_token(a):
                    return a.rearrange("p (t e) -> p t e", t=NT)

                def per_token(a):
                    return view(a, 0, [[1, NT], [0, NE]])

                dve.wait_ge(logits_ps, L + 1)
                lg = by_token(ps[:, 4, 0:NT * NE])
                done(v.tensor_reduce(r_t4, lg, AX.X, ALU.max))
                v.tensor_tensor(by_token(r_p), lg, per_token(r_t4), ALU.subtract).then_inc(logits_sub, 1)
                dve.wait_ge(logits_exp, L + 1)
                done(v.tensor_reduce(r_t4, by_token(r_p), AX.X, ALU.add))
                done(v.reciprocal(r_t4, r_t4))
                done(v.tensor_tensor(by_token(r_p), by_token(r_p), per_token(r_t4), ALU.mult))
                rank(r_rk, r_p, NT * NG)
                done(v.tensor_scalar(r_sel, r_rk, 2.0, None, ALU.is_lt))
                done(v.tensor_tensor(r_x, r_p, r_sel, ALU.mult))
                done(v.tensor_reduce(r_grp, r_x.rearrange("p (g e) -> p g e", e=EPG), AX.X, ALU.add))
                rank(r_grk, r_grp, NT)
                done(v.tensor_scalar(r_grk, r_grk, 1.0, None, ALU.is_lt))
                v.tensor_tensor(r_msk.rearrange("p (g e) -> p g e", e=EPG), r_sel.rearrange("p (g e) -> p g e", e=EPG),
                                view(r_grk, 0, [[1, NT * NG], [0, EPG]]), ALU.mult).then_inc(mask_done, 1)
                dve.wait_ge(mask_done, L + 1)
                done(v.tensor_tensor(r_x, r_p, r_msk, ALU.mult))
                done(v.tensor_reduce(r_t4, by_token(r_x), AX.X, ALU.add))
                done(v.reciprocal(r_t4, r_t4))
                done(v.tensor_tensor(by_token(r_x), by_token(r_x), per_token(r_t4), ALU.mult))
                dve.wait_ge(cum_ps, L + 1)
                done(v.tensor_copy(r_cnt, ps[:, 5, 64:64 + NE]))
                done(v.tensor_scalar(r_nbk, r_cnt, 0.0, None, ALU.is_gt))
                for k in range(1, NT):
                    done(v.scalar_tensor_tensor(r_nbk, r_cnt, float(k * P), r_nbk, ALU.is_gt, ALU.add))
                done(v.tensor_tensor_scan(r_end, ones[:, 0:NE], r_nbk, 0.0, ALU.mult, ALU.add))
                done(v.tensor_tensor(r_nbk, r_end, r_nbk, ALU.subtract))
                done(v.scalar_tensor_tensor(by_token(r_d), view(r_nbk, 0, [[0, NT], [1, NE]]), float(P),
                                            by_token(ps[:, 5, 0:NT * NE]), ALU.mult, ALU.add))
                done(v.tensor_tensor(r_d, r_d, r_msk, ALU.mult))
                done(v.tensor_scalar(r_sel, r_msk, -BIG, BIG, ALU.mult, ALU.add))
                done(v.tensor_tensor(r_sel, r_sel, r_d, ALU.add))
                for k, (d, op) in enumerate(((r_sel, ALU.min), (r_d, ALU.max))):
                    done(v.tensor_reduce(r_t4, by_token(d), AX.X, op))
                    v.tensor_copy(dst[:, :, k], r_t4)
                    done(v.tensor_tensor(by_token(r_rk), by_token(d), per_token(r_t4), ALU.is_equal))
                    done(v.tensor_tensor(r_rk, r_rk, r_x, ALU.mult))
                    done(v.tensor_reduce(gts[:, :, k], by_token(r_rk), AX.X, ALU.add))
                nbk = MAXB + 1
                b3 = view(r_blk[0:1], 0, [[NE, nbk], [1, NE]])
                done(v.tensor_tensor(b3, view(iota[0:1], 0, [[1, nbk], [0, NE]]), view(r_end[0:1], 0, [[0, nbk], [1, NE]]),
                                     ALU.is_ge))
                done(v.tensor_reduce(r_tb[0:1, 0:nbk], b3, AX.X, ALU.add))
                done(v.tensor_scalar(r_tb[0:1, 0:nbk], r_tb[0:1, 0:nbk], float(NE - 1), None, ALU.min))
                v.tensor_copy(r_tb[0:1, 24:25], r_end[0:1, NE - 1:NE])
                even = view(r_blk[0:1], 0, [[1, nbk]])
                done(v.tensor_scalar(even, iota[0:1, 0:nbk], 2.0, r_end[0:1, NE - 1:NE], ALU.mult, ALU.is_lt))
                done(v.tensor_reduce(r_tb[0:1, 25:26], even, AX.X, ALU.add))
                done(v.tensor_tensor(r_tb[0:1, 26:27], r_tb[0:1, 24:25], r_tb[0:1, 25:26], ALU.subtract))
                done(v.tensor_scalar(r_tb[0:1, 25:27], r_tb[0:1, 25:27], 16.0, None, ALU.mult))
                v.tensor_copy(tbl[0:1, 0:27], r_tb[0:1, 0:27]).then_inc(table_done, 1)

            def moe(L):
                dve.wait_ge(table_done, L + 1)
                nb = dve.value_load(tbl[0:1, 24:25], min_val=MINB, max_val=MAXB)

                def copy_rows(b):
                    for half in range(2):
                        dve.wait_ge(xgT_ps[L], b * 2 + half + 1)
                        v.tensor_copy(xgT[:, half * 4:half * 4 + 4, :],
                                      ps[:, 4 + half, :].rearrange("p (c n) -> p c n", c=4)).then_inc(xgT_done[L], 1)

                def hidden(b, first=False):
                    dve.wait_ge(sig_done[L], b + 1)
                    v.tensor_tensor(gs, sig, ps[:, 0, :], ALU.mult).then_inc(act_mul[L], 1)
                    dve.wait_ge(act_mul[L], b + 1)
                    dve.wait_ge(up_mm[L], b + 1)
                    if not first:
                        dve.wait_ge(hidT_ps[L], b)
                    v.tensor_tensor(hid, gs, ps[:, 1, :], ALU.mult).then_inc(hid_done[L], 1)

                def copy_hidden(b):
                    dve.wait_ge(hidT_ps[L], b + 1)
                    v.tensor_copy(hidT, ps[:, 6, :].rearrange("p (c n) -> p c n", c=NF)).then_inc(hidT_done[L], 1)

                copy_rows(0)
                hidden(0, first=True)
                copy_rows(1)
                copy_hidden(0)
                with dve.Fori(1, MAXB - 1, 1) as b:
                    with dve.If(b < nb):
                        hidden(b)
                        copy_rows(b + 1)
                        copy_hidden(b)
                with dve.Fori(MAXB - 1, MAXB, 1) as b:
                    with dve.If(b < nb):
                        hidden(b)
                        copy_hidden(b)

            norm(0, add_mixer(0))
            turn_copies(1)
            dve.wait_ge(xs_zeroed, 16 * 4)
            route(0)
            moe(0)
            norm(1, add_moe(0))
            turn_copies(2)

            def prepare(hd, first=False):
                dve.wait_ge(hproj_used, hd * 4 + 4)
                if not first:
                    dve.wait_ge(off_ps, hd * 2)
                    dve.wait_ge(hout_done, hd)
                lb, olb, nw = (col("lb", 0, 1), col("olb", 0, 1), prm[:, R_NW:R_NW + 1])
                lb, olb, nw = (a[:, bass.ds(hd, 1)] for a in (col("lb"), col("olb"), prm[:, R_NW:R_NW + HG]))
                v.tensor_scalar(FF, stg[:, 4:6, :], olb, lb, ALU.mult, ALU.add)
                v.tensor_scalar(K2, stg[:, 6:8, :], olb, None, ALU.mult)
                v.scalar_tensor_tensor(sg, stg[:, 2, :], nw, stg[:, 3, :], ALU.mult, ALU.mult)
                v.scalar_tensor_tensor(qs, stg[:, 0, :], float(P) ** -0.5, stg[:, 1, :], ALU.mult, ALU.mult
                                       ).then_inc(prep_in, 1)
                dve.wait_ge(prep_in, hd + 1)
                v.tensor_tensor(Q2, view(qs, 0, [[0, 2], [1, T]]), FF, ALU.mult)
                v.tensor_tensor(ksum, K2[:, 0, :], K2[:, 1, :], ALU.add).then_inc(prepped, 1)

            def segment_products(s):
                if s == 1:
                    return FF, 0, T
                return TL, 2 * T - 4 * T // s, T // s

            def update(hd, u):
                s = 1 << (u - 1)
                n = T // (2 * s)
                if u == 1:
                    dve.wait_ge(prepped, hd + 1)
                else:
                    dve.wait_ge(updated, hd * 8 + u - 1)
                    dve.wait_ge(level_done, hd * LEVELS + u - 1)
                src, at, step = segment_products(s)
                if u < 8:
                    to, at2, step2 = segment_products(2 * s)
                    v.tensor_tensor(view(to, at2, [[step2, 2], [1, n]]), view(src, at, [[step, 2], [2, n]]),
                                    view(src, at + 1, [[step, 2], [2, n]]), ALU.mult)
                if u < 8:
                    dve.wait_ge(gram_ps, hd * 8 + u + 1)
                else:
                    dve.wait_ge(off_ps, hd * 2 + 1)
                q, k = mixed(Q2, s, 0, T), mixed(K2, s, 0, T)
                v.tensor_tensor(q, q,
                                view(src, at + 1, [[2, n], [step - 1, 2], [0, s]]), ALU.mult)
                v.tensor_tensor(k, k,
                                view(src, at + step + 1, [[2, n], [-(step + 1), 2], [0, s]]), ALU.mult
                                ).then_inc(updated, 1)

            def pick(hd, level):
                if level == 1:
                    dve.wait_ge(masks_in, 16)
                    dve.wait_ge(diag_done, hd + 1)
                v.copy_predicated(diag, view(masks, (level - 1) * P, [[0, NT], [1, P]]),
                                  ps[:, 2 + level % 2, :].rearrange("p (c n) -> p c n", c=NT)).then_inc(level_done, 1)

            def head(hd, first=False):
                prepare(hd, first)
                for u in range(1, 9):
                    update(hd, u)
                    if u < 8:
                        pick(hd, u)
                dve.wait_ge(hpv_ps, hd + 1)
                v.tensor_tensor(OG[:, bass.ds(hd, 1), :].rearrange("p o t -> p (o t)"), ps[:, 7, :], sg, ALU.mult
                                ).then_inc(hout_done, 1)

            dve.wait_ge(masks_in, 16)
            head(0, first=True)
            with dve.Fori(1, HG, 1) as hd:
                head(hd)
            dve.wait_ge(ssq_ps, 1)
            v.tensor_scalar(col("rms"), ps[:, 0, 0:NT], 1.0 / D, RMS_EPS, ALU.mult, ALU.add).then_inc(rms_var, 1)
            dve.wait_ge(rms_std, 1)
            v.reciprocal(col("rms"), col("rms")).then_inc(rms_done, 1)
            norm(2, add_mixer(1))
            turn_copies(3)
            route(1)
            moe(1)
            norm(3, add_moe(1))

        @block.gpsimd
        def _(pool):
            pool.memset(zero, 0.0).then_inc(zero_set, 1)
            pool.memset(xrp[:, :, 0:2], 0.0)
            pool.memset(xrp[:, :, T + 2:PADC], 0.0).then_inc(pads_set, 1)
            pool.wait_ge(rotated, NT)
            pool.wait_ge(proj_used, 16)
            pool.tensor_tensor(gelu_tmp, gr, gr, ALU.mult).then_inc(pool_order, 1)
            pool.wait_ge(pool_order, 1)
            pool.tensor_scalar(gelu_tmp, gelu_tmp, 0.044715, 1.0, ALU.mult, ALU.add).then_inc(pool_order, 1)
            pool.wait_ge(pool_order, 2)
            pool.tensor_tensor(gelu_tmp, gelu_tmp, gr, ALU.mult).then_inc(gelu_arg, 1)
            pool.wait_ge(gelu_sig, 1)
            pool.tensor_tensor(gr, gr, gelu_tmp, ALU.mult).then_inc(gelu_done, 1)

            def moe(L):
                pool.wait_ge(table_done, L + 1)
                pool.wait_ge(xs_zeroed, 16 * 4)
                for t in range(NT):
                    for k in range(2):
                        pool.indirect_dma_start(xs, bass.IndirectOffsetOnAxis(ap=dst[:, t, k:k + 1], axis=0),
                                                h[:, t, :], None).then_inc(scattered, 16)
                n_even = pool.value_load(tbl[0:1, 25:26], min_val=16 * (MINB // 2), max_val=16 * MAXB)
                n_odd = pool.value_load(tbl[0:1, 26:27], min_val=16 * (MINB // 2), max_val=16 * MAXB)
                pool.wait_ge(scattered, (L + 1) * 16 * 2 * NT)
                pool.wait_ge(y_stored[L][0], n_even)
                pool.wait_ge(y_stored[L][1], n_odd)
                for t in range(NT):
                    for k in range(2):
                        pool.indirect_dma_start(Yg[:, 2 * t + k, :], None, xs,
                                                bass.IndirectOffsetOnAxis(ap=dst[:, t, k:k + 1], axis=0)
                                                ).then_inc(gathered, 16)

            moe(0)
            pool.wait_ge(v_done, 2 * NT)
            pool.memset(SQ, 0.0).then_inc(sq_zero, 1)

            def head(hd, first=False):
                pool.wait_ge(v_done, 2 * NT)
                if not first:
                    pool.wait_ge(hpv_ps, hd)
                pool.tensor_copy(vh, v1[:, :, bass.ds(hd * P, P)]).then_inc(vh_done, 1)
                for level in range(1, LEVELS + 1):
                    s = 1 << (level - 1)
                    if level == 1:
                        pool.wait_ge(prepped, hd + 1)
                    else:
                        pool.wait_ge(updated, hd * 8 + level - 1)
                    if level >= 3:
                        pool.wait_ge(gram_ps, hd * 8 + level - 1)
                    pool.tensor_tensor(view(km[level % 2], 0, [[2 * s, T // (2 * s)], [s, 2], [1, s]]),
                                       mixed(K2, s, 0, T), view(ones, 0, [[0, T // (2 * s)], [0, 2], [0, s]]), ALU.mult
                                       ).then_inc(keys_mixed, 1)
                pool.wait_ge(hsq_done, hd + 1)
                if first:
                    pool.wait_ge(sq_zero, 1)
                else:
                    pool.wait_ge(sq_added, hd)
                pool.tensor_tensor(SQ, SQ, sqt, ALU.add).then_inc(sq_added, 1)

            head(0, first=True)
            with pool.Fori(1, HG, 1) as hd:
                head(hd)
            moe(1)


_INS = ['x', 'w_in_even', 'w_out_even', 'lru_conv_w', 'lru_conv_b', 'lru_gate_w', 'lru_gate_b', 'lru_lambda',
        'w_in_odd', 'w_out_odd', 'hg_lower_bounds', 'hg_norm_w', 'ln_w', 'ln_b', 'router_w',
        'moe_w_gate', 'moe_w_up', 'moe_w_down']


def kernel(**inputs):
    import concourse.bacc as bacc
    from concourse.bass_utils import run_bass_kernel_spmd

    nc = bacc.Bacc("TRN2", target_bir_lowering=False, num_devices=1)
    arrays, args = {}, []
    everything = [(n, inputs[n]) for n in _INS] + sorted(constants().items())
    handles = {}
    for name, a in everything:
        a = np.ascontiguousarray(a)
        arrays[name] = a
        handles[name] = nc.dram_tensor(name, a.shape, mybir.dt.from_np(a.dtype), kind="ExternalInput").ap()
    handles["out"] = nc.dram_tensor("out", (1, T, D), F32, kind="ExternalOutput").ap()
    encoder_kernel(nc, **handles)
    r = run_bass_kernel_spmd(nc, [arrays], core_ids=[0])
    return r.results[0]["out"]
```

```python
from contextlib import ExitStack

import numpy as np
import concourse.bass as bass
from concourse import mybir

F32 = mybir.dt.float32
I32 = mybir.dt.int32
U32 = mybir.dt.uint32
ALU = mybir.AluOpType
ACT = mybir.ActivationFunctionType
AX = mybir.AxisListType

P = 128
D = 1024
T = 512
NT = T // P
ND = D // P
DEPTH = 2
HR, DKR = 4, 64
LRU_BLOCKS = 4
CONV = 4
HG = 8
NE, NG, EPG = 16, 4, 4
FE = 512
NF = FE // P
PADC = T + CONV
MAXX = (2 * T - 1) // P
ALPHA = float((2.0 * DEPTH) ** 0.25)
LN_EPS, RMS_EPS = 1e-5, 1e-6
GELU_C = 2.0 * float(np.sqrt(2.0 / np.pi))
BIG = 65536.0
LEVELS = 7
R_CW, R_CB, R_GB, R_LAM, R_LB, R_NW, NROWS = 0, 16, 20, 36, 44, 60, 68


def constants():
    f = np.float32
    inv = f(10000.0) ** (-np.arange(0, DKR, 2, dtype=f) / f(DKR))
    ang = np.arange(T, dtype=f)[:, None] * inv[None, :].astype(f)
    log_gamma = np.log1p(-(2.0 ** (-5.0 - np.arange(HR, dtype=np.float64))))
    u = np.arange(T + (NT - 1) * P)[None, None, :] - (NT - 1) * P - np.arange(P)[:, None, None]
    decay = np.exp(log_gamma[None, :, None] * np.abs(u)) * DKR ** -0.5
    j = np.arange(P)
    masks = np.zeros((P, LEVELS, P), np.int32)
    for level in range(LEVELS):
        s = 1 << level
        same = (j[:, None] // (2 * s)) == (j[None, :] // (2 * s))
        masks[:, level] = same & ((j[:, None] // s) != (j[None, :] // s))
    tri = np.concatenate([np.eye(P), np.ones((P, P)), j[:, None] < j[None, :]], axis=1)
    return {
        "c_rot": np.stack([np.cos(ang), np.sin(ang)], 1).astype(f),
        "c_decay": decay.astype(f),
        "c_masks": masks,
        "c_sq": tri.astype(f),
        "c_iota": np.tile(np.concatenate([np.arange(P), np.tri(EPG, k=-1).ravel()]).astype(f)[None, :], (P, 1)),
    }


def encoder_kernel(nc, x, w_in_even, w_out_even, lru_conv_w, lru_conv_b, lru_gate_w, lru_gate_b,
                   lru_lambda, w_in_odd, w_out_odd, hg_lower_bounds, hg_norm_w, ln_w, ln_b,
                   router_w, moe_w_gate, moe_w_up, moe_w_down,
                   c_rot, c_decay, c_masks, c_sq, c_iota, out):
    with ExitStack() as ctx:
        def sb(name, shape, dt=F32):
            return ctx.enter_context(nc.sbuf_tensor(name, shape, dt))

        def sem(name):
            return ctx.enter_context(nc.semaphore(name))

        h = sb("h", [P, NT, D])
        hT = sb("hT", [P, ND, T])
        W = sb("W", [P, 24576])
        S = sb("S", [P, 18432])
        sq = sb("sq", [P, 3, P])
        rw = sb("rw", [P, ND, NE])
        prm = sb("prm", [P, NROWS])
        rot = sb("rot", [P, NT, 2, DKR // 2])
        iota = sb("iota", [P, P + EPG * EPG])
        sm = sb("sm", [P, 512])
        dst = sb("dst", [P, NT, 2], U32)
        gts = sb("gts", [P, NT, 2])
        tbl = sb("tbl", [1, 16], I32)
        ident, ones, upper = sq[:, 0, :], sq[:, 1, :], sq[:, 2, :]
        ps = ctx.enter_context(nc.psum_tensor("ps", [P, 8, 512], F32))

        def S3(a, n, m):
            return S[:, a:a + n * m].rearrange("p (n m) -> p n m", n=n)

        def W3(a, n, m):
            return W[:, a:a + n * m].rearrange("p (n m) -> p n m", n=n)

        def view(base, start, dims):
            return bass.AP(base.tensor, base.offset + start, [list(base.ap[0])] + dims)

        names = {}
        for name, width in (("lam", 8), ("c", 8), ("negc", 8), ("w", 8), ("w2", 8), ("p", 8), ("lbm", 8),
                            ("lbe", 16), ("lb", 8), ("olb", 8), ("rms", 4), ("rvar", 16), ("rag", 32),
                            ("rst", 24), ("st", 12), ("ag", 8), ("std", 4), ("rst1", 4)):
            names[name] = (sum(w for _, w in names.values()), width)

        def col(name, first=0, n=None):
            a, width = names[name]
            return sm[:, a + first:a + (width if n is None else first + n)]

        qk, v0, g0 = S3(0, NT, 512), S3(2048, NT, 512), S3(4096, NT, 512)
        xrp, gr = S3(6144, NT, PADC), S3(8208, NT, 512)
        qkT, ret = S3(10256, NT, 512), S3(15888, NT, 512)
        decay = S3(12304, HR, 896)
        prob = [S3(0, NT, 512), S3(6144, NT, 512)]
        gelu_tmp = S3(15888, NT, 512)
        W_GROUPS = [0, 1536, 1024, 2048, 512]
        w_grp = [W3(4096 * n, ND, 512) for n in range(5)]
        zero, prm_rows = S[:, 17936:18192], S[:, 18192:18320]
        gate_w = W3(22528, 16, P)
        R = [W3(0, NT, 512), W3(4096, NT, 512)]
        IG = [W3(2048, NT, 512), W3(6144, NT, 512)]
        A_, TMP, xc = W3(8192, NT, 512), W3(10240, NT, 512), W3(20480, NT, 512)
        w_out0 = W3(12288, ND, D)
        mixT = hT
        OG = S3(8192, HG, T)
        v1 = W3(20480, NT, D)
        stg = W3(8192, 8, T)
        Q2, K2 = S3(12288, 2, T), S3(13312, 2, T)
        FF, TL = S3(14336, 2, T), S[:, 15360:16384]
        qs, sg, sqt, SQ = (S[:, 16384 + 512 * n:16896 + 512 * n] for n in range(4))
        ring = [W3(4096 * n, 4, ND * P).rearrange("p f (c n) -> p f c n", c=ND) for n in range(2)]
        w_v1, w_out1 = S3(0, ND, D), S3(0, ND, D)
        attn = W3(12288, NT, T)
        ksum = W[:, 14336:14848]
        masks = W[:, 14848:14848 + LEVELS * P].bitcast(I32).rearrange("p (l n) -> p l n", l=LEVELS)
        vh = W3(15744, NT, P)
        km = [W[:, 16256 + 512 * n:16768 + 512 * n] for n in range(2)]
        places = [W[:, 0:12288], W[:, 12288:24576], S[:, 0:12288]]
        places = [[places[n] for n in order] for order in ((0, 2, 1), (0, 1, 2))]
        wg, wu, wd = ([[w[:, a:a + 4096].rearrange("p (n m) -> p n m", n=n) for w in layer] for layer in places]
                      for a, n in ((0, ND), (4096, ND), (8192, NF)))
        xg = [S[:, 12288 + 1024 * n:13312 + 1024 * n] for n in range(3)]
        first_sel = S3(12288, NT, P)
        xgT = S3(15360, ND, P)
        scratch = hT[:].rearrange("p c n -> p (c n)")
        sig, gs, hid = (scratch[:, 512 * n:512 * n + 512] for n in range(3))
        hidT = scratch[:, 1536:2048].rearrange("p (n m) -> p n m", n=NF)
        yo = [scratch[:, 2048 + 1024 * n:3072 + 1024 * n] for n in range(2)]
        Yg = W3(0, NT * 2, D)
        lnw, lnb = S[:, 14336:15360], S[:, 16384:17408]
        rt = S[:, 17408:18432]
        ysc = S3(12288, 2, 512)

        xs = nc.dram_tensor("slot_rows", [(NE + MAXX) * P, D], F32, kind="Internal").ap()
        rows = "(c p) n -> p c n"

        r_at = [0]

        def r_(n):
            r_at[0] += n
            return rt[:, r_at[0] - n:r_at[0]]

        r_p, r_rk, r_sel, r_x, r_d, r_over = (r_(NT * NE) for _ in range(6))
        r_msk5 = r_((NT + 1) * NE)
        r_msk = r_msk5[:, 0:NT * NE]
        r_gt, r_ge = r_(NT * NE * EPG), S[:, 15360:15360 + NT * NE * EPG]
        r_t4, r_grp, r_grk, r_nbk, r_end, r_tb = (
            r_(n) for n in (NT, NT * NG, NT * NG, NE, NE, 16))
        r_skip = r_(NE)
        r_blk = r_gt[:, 0:MAXX * NE]
        T_NX, T_STORES = 8, 9
        diag = view(attn, 0, [[T + P, NT], [1, P]])
        neighbours = view(attn, P, [[2 * T + 2 * P, 2], [T - P, 2], [1, P]])

        def sems(name, n):
            return [sem(f"{name}_{i}") for i in range(n)]

        x_in = sems("x_in", NT)
        sq_in, prm_in, tab_in, gatew_in = (sem(n) for n in ("sq_in", "prm_in", "tab_in", "gatew_in"))
        win_in, wout_in, lnp_in = sems("win_in", 6), sem("wout_in"), sem("lnp_in")
        zero_set, xs_zeroed, pads_set = sem("zero_set"), sem("xs_zeroed"), sem("pads_set")
        ring_in, wv_in, masks_in = sems("ring_in", 2), sem("wv_in"), sem("masks_in")
        xg_in, wgu_in, wd_in = ([sems(f"{k}_in{L}", 3) for L in range(2)] for k in ("xg", "wgu", "wd"))
        prmT, prmC = sem("prm_turned"), sem("prm_copied")
        hT_ps, hT_done = sem("hT_in_psum"), sem("hT_copied")
        proj, proj_used, g_sigm, g_used = sem("proj"), sem("proj_used"), sem("g_sigmoid"), sem("g_used")
        rotated, qkT_ps, qkT_done = sem("rotated"), sem("qkT_in_psum"), sem("qkT_copied")
        conv_done, gate_ps, gate_done = sem("conv_done"), sem("gate_in_psum"), sem("gate_done")
        score_ps, prob_done, pv_ps = sem("score_in_psum"), sem("prob_done"), sem("pv_in_psum")
        lam_abs, lam_exp, lam_c = sem("lam_abs"), sem("lam_exp"), sem("lam_c")
        lb_sub, lb_exp = sem("lb_sub"), sem("lb_exp")
        a_done, tanh_done, ratio, ratio_sqrt, scanned = (sem(n) for n in (
            "a_done", "tanh_done", "ratio", "ratio_sqrt", "scanned"))
        gelu_arg, gelu_sig, gelu_done = sem("gelu_arg"), sem("gelu_sig"), sem("gelu_done")
        lru_done, ret_var, ret_std, ret_done, retT_ps, retT_done = (sem(n) for n in (
            "lru_done", "ret_var", "ret_std", "ret_done", "retT_in_psum", "retT_done"))
        op_ps, op_used, op_added = sem("outproj"), sem("outproj_used"), sem("outproj_added")
        var_done, std_done, ln_done = sem("ln_var"), sem("ln_std"), sem("ln_done")
        standard, affine, h_scaled = sem("standardised"), sem("ln_scaled"), sem("h_scaled")
        logits_ps, logits_sub, logits_exp, mask_done, cum_ps, slots_done, sel_done, table_done = (sem(k) for k in (
            "logits_in_psum", "logits_sub", "logits_exp", "mask_done", "cum_in_psum", "slots_done", "sel_done",
            "table_done"))
        scattered, gathered = sem("scattered"), sems("gathered", NT)
        xgT_ps, xgT_done, gate_mm, up_mm, sig_done, act_mul, hid_done, hidT_ps, hidT_done, down_mm, y_copied = (
            sems(k, 2) for k in ("xgT_in_psum", "xgT_done", "gate_mm", "up_mm", "sig_done", "act_mul", "hid_done",
                                 "hidT_in_psum", "hidT_done", "down_mm", "y_copied"))
        y_stored = [sems(f"y_stored{L}", 2) for L in range(2)]
        v_ps, v_done, vh_done = sem("v_in_psum"), sem("v_copied"), sem("vh_copied")
        hproj, hproj_used, staged = sem("hproj"), sem("hproj_used"), sem("staged")
        prep_in, prepped, updated = sem("prep_inputs"), sem("prepped"), sem("updated")
        gram_ps, diag_done, level_done = sem("gram_in_psum"), sem("diag_done"), sem("level_done")
        off_ps, off_done = sem("off_in_psum"), sem("off_done")
        hpv_ps, hout_done, hsq_done, sq_added, sq_zero = (sem(n) for n in (
            "hpv_in_psum", "hout_done", "hsq_done", "sq_added", "sq_zeroed"))
        keys_updated, keys_mixed = sem("keys_updated"), sem("keys_mixed")
        ssq_ps, rms_var, rms_std, rms_done = sem("ssq_in_psum"), sem("rms_var"), sem("rms_std"), sem("rms_done")
        stored = sem("out_stored")
        dve_order, pool_order = sem("dve_order"), sem("pool_order")

        block = ctx.enter_context(nc.Block())

        def mixed(buf, s, first, n):
            return view(buf, first, [[2 * s, n // (2 * s)], [T + s, 2], [1, s]])

        @block.sync
        def _(sp):
            sp.dma_start(sq[:], c_sq.rearrange("p (a n) -> p a n", a=3)).then_inc(sq_in, 16)
            for t in range(NT):
                sp.dma_start(h[:, t, :], x[0, t * P:(t + 1) * P, :]).then_inc(x_in[t], 16)
            for n, first in enumerate(W_GROUPS):
                src = w_in_even[0][:, first:first + 512].rearrange(rows, p=P)
                if n == 0:
                    sp.dma_start(w_grp[0][:, 0:4, :], src[:, 0:4, :]).then_inc(win_in[5], 16)
                    sp.dma_start(w_grp[0][:, 4:8, :], src[:, 4:8, :]).then_inc(win_in[0], 16)
                else:
                    sp.dma_start(w_grp[n], src).then_inc(win_in[n], 16)
            sp.dma_start(gate_w, lru_gate_w[0].rearrange("z g n c d -> c (z g n) d")).then_inc(gatew_in, 16)
            sp.wait_ge(proj, 20)
            sp.dma_start(w_out0, w_out_even[0].rearrange(rows, p=P)).then_inc(wout_in, 16)

            def norm_scale(n):
                sp.dma_start(lnw, ln_w[n // 2, n % 2].partition_broadcast(P)).then_inc(lnp_in, 16)

            def norm_shift(n):
                sp.dma_start(lnb, ln_b[n // 2, n % 2].partition_broadcast(P)).then_inc(lnp_in, 16)

            wgl, wul, wdl = (w.rearrange("l e (c p) n -> l e p c n", p=P) for w in (moe_w_gate, moe_w_up, moe_w_down))
            xsb = xs.rearrange("(b p) d -> b p d", p=P)

            def expert(w, L, e):
                return w[L, bass.ds(e, 1)].rearrange("o p c n -> p (o c) n")

            def load_gate_up(L, e, k):
                sp.dma_start(wg[L][k], expert(wgl, L, e)).then_inc(wgu_in[L][k], 16)
                sp.dma_start(wu[L][k], expert(wul, L, e)).then_inc(wgu_in[L][k], 16)

            def load_down(L, e, k):
                sp.dma_start(wd[L][k], expert(wdl, L, e)).then_inc(wd_in[L][k], 16)

            def load_rows(L, b, k):
                sp.dma_start(xg[k], xsb[bass.ds(b, 1)].rearrange("o p d -> p (o d)")).then_inc(xg_in[L][k], 16)

            def moe_loads(L):
                sp.wait_ge(scattered, (L + 1) * 16 * 2 * NT)
                for k in (1, 2):
                    load_rows(L, k, k)

                def load(b, k):
                    sp.wait_ge(up_mm[L], b)
                    load_gate_up(L, b + 2, k)
                    sp.wait_ge(down_mm[L], b * 2)
                    load_down(L, b + 2, k)

                def next_rows(b, k):
                    sp.wait_ge(xgT_ps[L], b * 2)
                    load_rows(L, b + 2, k)

                with sp.Fori(1, NE - 5, 3) as b:
                    for i in range(3):
                        next_rows(b + i, i)
                        load(b + i, i)
                next_rows(NE - 3, 0)
                load(NE - 3, 0)
                if L == 0:
                    sp.wait_ge(down_mm[0], (NE - 2) * 2)
                    sp.dma_start(w_v1, w_in_odd[0][:, D:2 * D].rearrange(rows, p=P)).then_inc(wv_in, 16)
                sp.wait_ge(xgT_ps[L], (NE - 1) * 2)
                norm_scale(2 * L + 1)
                norm_shift(2 * L + 1)
                sp.wait_ge(table_done, L + 1)
                nx = sp.value_load(tbl[0:1, T_NX:T_NX + 1], min_val=0, max_val=MAXX)
                with sp.Fori(0, MAXX, 1) as j:
                    with sp.If(j < nx):
                        e = sp.value_load(tbl[0:1, bass.ds(j, 1)], min_val=0, max_val=NE - 1)
                        sp.wait_ge(down_mm[L], (j + NE) * 2)
                        load_rows(L, j + NE, 0)
                        load_gate_up(L, e, 0)
                        load_down(L, e, 0)

            sp.wait_ge(lru_done, 1)
            load_gate_up(0, 0, 0)
            load_down(0, 0, 0)
            sp.wait_ge(retT_ps, HR)
            norm_scale(0)
            norm_shift(0)
            load_gate_up(0, 1, 1)
            load_down(0, 1, 1)
            sp.wait_ge(op_ps, 2 * NT)
            load_gate_up(0, 2, 2)
            load_down(0, 2, 2)
            moe_loads(0)

            w5 = w_in_odd[0].rearrange("(c p) (f h n) -> f h p c n", p=P, f=5, h=HG)

            def head_weights(hd, slot):
                for n, f in enumerate((0, 2, 3, 4)):
                    sp.dma_start(ring[slot][:, n], w5[f, bass.ds(hd, 1)].rearrange("o p c n -> p (o c) n")
                                 ).then_inc(ring_in[slot], 16)

            sp.wait_ge(ln_done, 2 * NT)
            head_weights(0, 0)
            sp.dma_start(masks, c_masks).then_inc(masks_in, 16)
            head_weights(1, 1)
            sp.wait_ge(v_ps, 2 * NT)
            sp.dma_start(w_out1, w_out_odd[0].rearrange(rows, p=P)).then_inc(wout_in, 16)
            with sp.Fori(2, HG - 1, 2) as hd:
                for k in range(2):
                    sp.wait_ge(hproj, (hd + k - 1) * 4)
                    head_weights(hd + k, k)
            sp.wait_ge(hout_done, HG)
            norm_scale(2)
            norm_shift(2)
            for k in range(2):
                load_gate_up(1, k, k)
                load_down(1, k, k)
            sp.wait_ge(op_ps, 4 * NT)
            load_gate_up(1, 2, 2)
            load_down(1, 2, 2)
            moe_loads(1)
            for t in range(NT):
                sp.wait_ge(ln_done, 3 * NT + t + 1)
                sp.dma_start(out[0, t * P:(t + 1) * P, :], h[:, t, :]).then_inc(stored, 16)
            sp.wait_ge(stored, 16 * NT)

        @block.tensor
        def _(pe):
            def turn_h(n, t):
                if n == 0:
                    pe.wait_ge(x_in[t], 16)
                else:
                    pe.wait_ge(ln_done, (n - 1) * NT + t + 1)
                for half in range(2):
                    for c in range(4):
                        last = pe.transpose(ps[:, 2 * t + half, c * P:(c + 1) * P],
                                            h[:, t, (half * 4 + c) * P:(half * 4 + c + 1) * P], ident)
                    last.then_inc(hT_ps, 1)

            pe.wait_ge(sq_in, 16)
            for t in range(NT):
                turn_h(0, t)
            pe.wait_ge(hT_done, 2 * NT)

            def project(n):
                grp, i = n // 4, n % 4
                if i == 0:
                    pe.wait_ge(win_in[5 if n == 0 else grp], 16)
                if n >= 16:
                    pe.wait_ge(proj_used, n - 7)
                elif n >= 12:
                    pe.wait_ge(g_used, n - 11)
                elif n >= 4:
                    pe.wait_ge(proj_used, n - 3)
                for c in range(ND):
                    if n == 0 and c == 4:
                        pe.wait_ge(win_in[0], 16)
                    if grp in (1, 3):
                        a, b = w_grp[grp][:, c, i * P:(i + 1) * P], hT[:, c, :]
                    else:
                        a, b = hT[:, c, i * P:(i + 1) * P], w_grp[grp][:, c, :]
                    last = pe.matmul(ps[:, 4 + n % 4, :], a, b, start=(c == 0), stop=(c == ND - 1))
                last.then_inc(proj, 1)

            for n in range(4):
                project(n)
            pe.wait_ge(prm_in, 16 * 6)
            pe.transpose(ps[:, 0, 0:NROWS], prm_rows[0:NROWS], ident[0:NROWS, 0:NROWS]
                         ).then_inc(prmT, 1)
            for n in range(4, 8):
                project(n)
            pe.wait_ge(prmC, 1)
            for t in range(NT):
                pe.wait_ge(rotated, t + 1)
                for c in range(4):
                    last = pe.transpose(ps[:, t, c * P:(c + 1) * P], qk[:, t, c * P:(c + 1) * P], ident)
                last.then_inc(qkT_ps, 1)
            for n in range(8, 12):
                project(n)
            pe.wait_ge(qkT_done, NT)
            pe.wait_ge(gatew_in, 16)
            pe.wait_ge(conv_done, NT)
            for k in range(16):
                n, zg = k // 4, k % 4
                if k >= 4:
                    pe.wait_ge(gate_done, k - 3)
                pe.matmul(ps[:, k % 4, :], gate_w[:, zg * 4 + n, :], xc[:, n, :], start=True, stop=True
                          ).then_inc(gate_ps, 1)
            for n in range(12, 20):
                project(n)

            def scores(hd):
                lo = DKR * (hd % 2)
                for j in range(NT):
                    if hd == 0:
                        pe.wait_ge(gate_done, 13 + j)
                    else:
                        pe.wait_ge(prob_done, (hd - 1) * NT + j + 1)
                    pe.matmul(ps[:, j, :], qkT[lo:lo + DKR, 2 + hd // 2, j * P:(j + 1) * P],
                              qkT[lo:lo + DKR, hd // 2, :], start=True, stop=True).then_inc(score_ps, 1)

            scores(0)
            pe.wait_ge(proj_used, 16)
            for hd in range(HR):
                if hd + 1 < HR:
                    scores(hd + 1)
                pe.wait_ge(prob_done, (hd + 1) * NT)
                for t in range(NT):
                    for j in range(NT):
                        last = pe.matmul(ps[:, 4 + hd, t * P:(t + 1) * P], prob[hd % 2][:, j, t * P:(t + 1) * P],
                                         v0[:, j, hd * P:(hd + 1) * P], start=(j == 0), stop=(j == NT - 1))
                last.then_inc(pv_ps, 1)

            def out_project(k, srcT, w, tiles, start, stop):
                t, half = k // 2, k % 2
                for c in tiles:
                    last = pe.matmul(ps[:, k, :], srcT[:, c, t * P:(t + 1) * P], w[:, c, half * 512:(half + 1) * 512],
                                     start=(start and c == tiles[0]), stop=(stop and c == tiles[-1]))
                return last

            def logits(L, t):
                pe.wait_ge(hT_done, (2 * L + 1) * 2 * NT + 2 * t + 2)
                for c in range(ND):
                    last = pe.matmul(ps[:, 0, t * NE:(t + 1) * NE], hT[:, c, t * P:(t + 1) * P], rw[:, c, :],
                                     start=(c == 0), stop=(c == ND - 1))
                last.then_inc(logits_ps, 1)

            def router(L):
                pe.wait_ge(mask_done, L + 1)
                pe.matmul(ps[:, 1, 0:(NT + 1) * NE], upper, r_msk5, start=True, stop=False)
                for u in range(NT):
                    last = pe.matmul(ps[:, 1, (u + 1) * NE:(NT + 1) * NE], ones,
                                     view(r_msk5, u * NE, [[0, NT - u], [1, NE]]), start=False, stop=(u == NT - 1))
                last.then_inc(cum_ps, 1)

            def moe(L):

                def turn_rows(k, loads):
                    pe.wait_ge(xg_in[L][k], loads if k else loads - 16)
                    for half in range(2):
                        for c in range(4):
                            last = pe.transpose(ps[:, 4 + half, c * P:(c + 1) * P],
                                                xg[k][:, (half * 4 + c) * P:(half * 4 + c + 1) * P], ident)
                        last.then_inc(xgT_ps[L], 1)

                def gate_up(b, k, loads):
                    pe.wait_ge(xgT_done[L], (b + 1) * 2)
                    pe.wait_ge(wgu_in[L][k], loads * 2)
                    for bank, w, done in ((0, wg, gate_mm), (1, wu, up_mm)):
                        for c in range(ND):
                            last = pe.matmul(ps[:, bank, :], xgT[:, c, :], w[L][k][:, c, :],
                                             start=(c == 0), stop=(c == ND - 1))
                        last.then_inc(done[L], 1)

                def turn_hidden(b):
                    pe.wait_ge(hid_done[L], b + 1)
                    for c in range(NF):
                        last = pe.transpose(ps[:, 6, c * P:(c + 1) * P], hid[:, c * P:(c + 1) * P], ident)
                    last.then_inc(hidT_ps[L], 1)

                def down(b, k, loads, first=False):
                    pe.wait_ge(wd_in[L][k], loads)
                    pe.wait_ge(hidT_done[L], b + 1)
                    if not first:
                        pe.wait_ge(y_copied[L], b * 2)
                    for half in range(2):
                        for c in range(NF):
                            last = pe.matmul(ps[:, 2 + half, :], hidT[:, c, :],
                                             wd[L][k][:, c, half * 512:(half + 1) * 512],
                                             start=(c == 0), stop=(c == NF - 1))
                        last.then_inc(down_mm[L], 1)

                def step(b, k, loads, last=False, first=False):
                    gate_up(b, k, loads)
                    if not last:
                        turn_rows((k + 1) % 3, loads if k < 2 else loads + 16)
                    down(b - 1, (k - 1) % 3, loads if k else loads - 16, first)
                    turn_hidden(b)

                pe.wait_ge(sel_done, L + 1)
                for half in range(2):
                    for c in range(4):
                        for t in range(NT):
                            last = pe.matmul(ps[:, 4 + half, c * P:(c + 1) * P],
                                             h[:, t, (half * 4 + c) * P:(half * 4 + c + 1) * P], first_sel[:, t, :],
                                             start=(t == 0), stop=(t == NT - 1))
                    last.then_inc(xgT_ps[L], 1)
                gate_up(0, 0, 16)
                turn_rows(1, 16)
                turn_hidden(0)
                step(1, 1, 16, first=True)
                step(2, 2, 16)
                with pe.Fori(1, NE // 3, 1) as r:
                    for k in range(3):
                        step(r * 3 + k, k, (r + 1) * 16)
                step(NE - 1, 0, (NE // 3 + 1) * 16, last=True)
                down(NE - 1, 0, (NE // 3 + 1) * 16)
                pe.wait_ge(table_done, L + 1)
                nx = pe.value_load(tbl[0:1, T_NX:T_NX + 1], min_val=0, max_val=MAXX)
                with pe.Fori(0, MAXX, 1) as j:
                    with pe.If(j < nx):
                        turn_rows(0, (j + (NE // 3 + 2)) * 16)
                        gate_up(j + NE, 0, (j + (NE // 3 + 2)) * 16)
                        turn_hidden(j + NE)
                        down(j + NE, 0, (j + (NE // 3 + 2)) * 16)

            pe.wait_ge(lru_done, 1)
            pe.wait_ge(wout_in, 16)
            for k in range(NT):
                pe.wait_ge(prob_done, (HR - 1) * NT + k + 1)
                out_project(k, mixT, w_out0, range(4, 8), True, False)
            for hd in range(HR):
                pe.wait_ge(ret_done, hd + 1)
                for t in range(NT):
                    last = pe.transpose(ps[:, 4 + hd, t * P:(t + 1) * P], ret[:, t, hd * P:(hd + 1) * P], ident)
                last.then_inc(retT_ps, 1)
            pe.wait_ge(retT_done, HR)
            for k in range(2 * NT):
                if k < NT:
                    out_project(k, mixT, w_out0, range(4), False, True).then_inc(op_ps, 1)
                else:
                    out_project(k, mixT, w_out0, range(ND), True, True).then_inc(op_ps, 1)
                if k == 5:
                    turn_h(1, 0)
                if k == 6:
                    logits(0, 0)
                    turn_h(1, 1)
            for t in range(2, NT):
                turn_h(1, t)
                logits(0, t - 1)
            logits(0, NT - 1)
            router(0)
            moe(0)

            pe.wait_ge(wv_in, 16)
            turn_h(2, 0)
            for t in range(NT):
                pe.wait_ge(hT_done, 4 * NT + 2 * t + 2)
                for k in (2 * t, 2 * t + 1):
                    if k % 2 and t + 1 < NT:
                        turn_h(2, t + 1)
                    for c in range(ND):
                        last = pe.matmul(ps[:, k, :], hT[:, c, t * P:(t + 1) * P],
                                         w_v1[:, c, (k % 2) * 512:(k % 2 + 1) * 512], start=(c == 0), stop=(c == ND - 1))
                    last.then_inc(v_ps, 1)
            pe.wait_ge(v_done, 2 * NT)

            def head_project(hd, slot, f, tiles, first=False):
                if tiles[0] == 0:
                    if f == 0:
                        pe.wait_ge(ring_in[slot], (hd - slot + 2) * 32)
                    if not first or f >= 2:
                        pe.wait_ge(hproj_used, hd * 4 + f - 1)
                for c in tiles:
                    last = pe.matmul(ps[:, f % 2, :], ring[slot][:, f, c, :], hT[:, c, :],
                                     start=(c == 0), stop=(c == ND - 1))
                if tiles[-1] == ND - 1:
                    last.then_inc(hproj, 1)

            def gram(hd, level):
                if level == 0:
                    pe.wait_ge(prepped, hd + 1)
                if level == 2:
                    pe.wait_ge(diag_done, hd + 1)
                if level >= 1:
                    pe.wait_ge(keys_mixed, hd * LEVELS + level)
                if level >= 2:
                    pe.wait_ge(updated, hd * 8 + level - 1)
                if level >= 3:
                    pe.wait_ge(level_done, hd * LEVELS + level - 2)
                for c in range(NT):
                    o = ps[:, 2 + level % 2, c * P:(c + 1) * P]
                    if level == 0:
                        last = pe.matmul(o, ksum[:, c * P:(c + 1) * P], qs[:, c * P:(c + 1) * P], start=True, stop=True)
                    else:
                        s = 1 << (level - 1)
                        last = pe.matmul(o, km[level % 2][:, c * P:(c + 1) * P], mixed(Q2, s, c * P, P), start=True, stop=True)
                last.then_inc(gram_ps, 1)

            def gram_off(hd):
                pe.wait_ge(updated, hd * 8 + 7)
                for j in range(NT):
                    i = j ^ 1
                    last = pe.matmul(ps[:, 4, j * P:(j + 1) * P], K2[:, j % 2, j * P:(j + 1) * P],
                                     Q2[:, i % 2, i * P:(i + 1) * P], start=True, stop=True)
                last.then_inc(off_ps, 1)

            def gram_pairs(hd):
                pe.wait_ge(updated, hd * 8 + 8)
                for j in range(NT):
                    i = 1 - j // 2
                    last = pe.matmul(ps[:, 5 + j // 2, (j % 2) * 256:(j % 2 + 1) * 256],
                                     K2[:, j // 2, j * P:(j + 1) * P],
                                     Q2[:, i, i * 256:(i + 1) * 256], start=True, stop=True)
                last.then_inc(off_ps, 1)

            def head_pv(hd, first=False):
                pe.wait_ge(level_done, hd * LEVELS + LEVELS)
                pe.wait_ge(off_done, hd * 2 + 2)
                pe.wait_ge(vh_done, hd + 1)
                if not first:
                    pe.wait_ge(hsq_done, hd)
                for j in range(NT):
                    last = pe.matmul(ps[:, 7, :], vh[:, j, :], attn[:, j, :], start=(j == 0), stop=(j == NT - 1))
                last.then_inc(hpv_ps, 1)

            def attend(hd, slot, first=False):
                if slot is not None:
                    parts = [(f, range(a, a + 2)) for f in range(4) for a in (0, 2, 4, 6)]
                else:
                    parts = [(k, range(a, min(a + 2, HG - 1))) for k in range(2) for a in (0, 2, 4, 6)]

                def fill(n=1):
                    for _ in range(n):
                        if not parts:
                            return
                        f, tiles = parts.pop(0)
                        if slot is not None:
                            head_project(hd + 1, slot, f, tiles)
                        else:
                            out_project(f, OG, w_out1, tiles, tiles[0] == 0, False)

                fill(4 if slot is not None else 1)
                for level in range(LEVELS + 1):
                    gram(hd, level)
                    if level > 0:
                        fill(2 if level <= 3 and slot is not None else 1)
                gram_off(hd)
                fill()
                gram_pairs(hd)
                fill()
                head_pv(hd, first)

            for f in range(4):
                head_project(0, 0, f, range(ND), first=True)
            attend(0, 1, first=True)
            attend(1, 0)
            with pe.Fori(2, HG - 3, 2) as hd:
                attend(hd, 1)
                attend(hd + 1, 0)
            attend(HG - 2, 1)
            pe.wait_ge(wout_in, 32)
            pe.wait_ge(hproj_used, 4 * HG)
            pe.wait_ge(hout_done, HG - 1)
            attend(HG - 1, None)
            pe.wait_ge(level_done, HG * LEVELS)
            pe.wait_ge(off_done, HG * 2)
            for k in (2, 3):
                out_project(k, OG, w_out1, range(HG - 1), True, False)
            pe.wait_ge(hout_done, HG)
            for k in range(2 * NT):
                if k == 4:
                    pe.wait_ge(sq_added, HG)
                    for t in range(NT):
                        last = pe.matmul(ps[:, 7, t:t + 1], SQ[:, t * P:(t + 1) * P], ones[:, 0:1], start=True, stop=True)
                    last.then_inc(ssq_ps, 1)
                if k < 4:
                    out_project(k, OG, w_out1, range(HG - 1, HG), False, True).then_inc(op_ps, 1)
                else:
                    if k == 7:
                        pe.wait_ge(rms_var, 1)
                    out_project(k, OG, w_out1, range(HG), True, True).then_inc(op_ps, 1)
                if k == 5:
                    turn_h(3, 0)
                if k == 6:
                    logits(1, 0)
                    turn_h(3, 1)
            for t in range(2, NT):
                turn_h(3, t)
                logits(1, t - 1)
            logits(1, NT - 1)
            router(1)
            moe(1)

        @block.scalar
        def _(act):
            def copy(o, i):
                return nc.scalar.activation(o, i, ACT.Copy)

            def turn_copies(n, t):
                for k in (2 * t, 2 * t + 1):
                    act.wait_ge(hT_ps, n * 2 * NT + k + 1)
                    copy(hT[:, 4 * (k % 2):4 * (k % 2) + 4, t * P:(t + 1) * P],
                         ps[:, k, :].rearrange("p (c n) -> p c n", c=4)).then_inc(hT_done, 1)

            for first, a, n in ((R_CW, lru_conv_w[0].rearrange("j (b c) -> (j b) c", c=P), 16),
                                (R_CB, lru_conv_b[0].rearrange("(b c) -> b c", c=P), 4),
                                (R_GB, lru_gate_b[0].rearrange("z g n c -> (z g n) c"), 16),
                                (R_LAM, lru_lambda[0].rearrange("z (b c) -> (z b) c", c=P), 8),
                                (R_LB, hg_lower_bounds.rearrange("l (b c) -> (l b) c", c=P), 16),
                                (R_NW, hg_norm_w[0].rearrange("(b c) -> b c", c=P), 8)):
                act.dma_start(prm_rows[first:first + n], a).then_inc(prm_in, 16)
            act.dma_start(rot[:], c_rot.rearrange("(n p) a k -> p n a k", p=P)).then_inc(tab_in, 16)
            act.dma_start(rw[:], router_w.rearrange(rows, p=P)).then_inc(tab_in, 16)
            act.dma_start(iota[:], c_iota).then_inc(tab_in, 16)
            act.dma_start(decay, c_decay).then_inc(tab_in, 16)
            for t in range(NT):
                turn_copies(0, t)

            def projected(n):
                grp, i = n // 4, n % 4
                act.wait_ge(proj, n + 1)
                bank = ps[:, 4 + n % 4, :]
                if grp == 2:
                    nc.scalar.activation(g0[:, i, :], bank, ACT.Sigmoid).then_inc(g_sigm, 1)
                else:
                    to = {0: qk[:, i, :], 1: xrp[:, i, 2:2 + T], 3: gr[:, i, :], 4: v0[:, i, :]}[grp]
                    copy(to, bank).then_inc(proj_used, 1)

            for n in range(4):
                projected(n)
            act.wait_ge(prmT, 1)
            copy(prm[:], ps[:, 0, 0:NROWS]).then_inc(prmC, 1)
            act.wait_ge(zero_set, 1)
            zrows = xs.rearrange("(p b) (q e) -> p (b q) e", p=P, e=256)
            for n in range(4):
                act.dma_start(zrows[:, n * (NE + MAXX):(n + 1) * (NE + MAXX), :],
                              view(zero, 0, [[0, NE + MAXX], [1, 256]])).then_inc(xs_zeroed, 16)
            act.wait_ge(pads_set, 1)
            for n in range(4, 8):
                projected(n)
            act.wait_ge(lam_abs, 1)
            nc.scalar.activation(col("lam"), col("lam"), ACT.Exp, scale=-1.0).then_inc(lam_exp, 1)
            act.wait_ge(lb_sub, 1)
            nc.scalar.activation(col("lbe"), col("lbe"), ACT.Exp).then_inc(lb_exp, 1)
            for n in range(8, 12):
                projected(n)
            for k in range(16):
                n, zg = k // 4, k % 4
                act.wait_ge(gate_ps, k + 1)
                nc.scalar.activation((R, IG)[zg % 2][zg // 2][:, n, :], ps[:, k % 4, :], ACT.Sigmoid,
                                     bias=prm[:, R_GB + zg * 4 + n:R_GB + zg * 4 + n + 1]).then_inc(gate_done, 1)
            act.wait_ge(lam_c, 1)
            act.wait_ge(gate_done, 16)

            def decays(z):
                if z == 1:
                    act.wait_ge(scanned, 1)
                for n in range(NT):
                    last = nc.scalar.activation(A_[:, n, :], R[z][:, n, :], ACT.Exp, scale=col("negc", z * 4 + n, 1))
                last.then_inc(a_done, 1)
                act.wait_ge(a_done, z + 1)
                for n in range(NT):
                    last = nc.scalar.activation(R[z][:, n, :], R[z][:, n, :], ACT.Tanh, scale=col("c", z * 4 + n, 1))
                last.then_inc(tanh_done, 1)

            def ratio_root(z):
                act.wait_ge(ratio, z + 1)
                nc.scalar.activation(TMP, TMP, ACT.Sqrt).then_inc(ratio_sqrt, 1)

            decays(0)
            projected(12)
            projected(13)
            ratio_root(0)
            projected(14)
            projected(15)
            decays(1)
            projected(16)
            ratio_root(1)
            projected(17)
            act.wait_ge(gelu_arg, 1)
            nc.scalar.activation(gelu_tmp, gelu_tmp, ACT.Sigmoid, scale=GELU_C).then_inc(gelu_sig, 1)
            projected(18)
            projected(19)
            for hd in range(HR):
                act.wait_ge(ret_var, hd + 1)
                nc.scalar.activation(col("rvar", hd * NT, NT), col("rvar", hd * NT, NT), ACT.Sqrt).then_inc(ret_std, 1)
            for hd in range(HR):
                act.wait_ge(retT_ps, hd + 1)
                copy(mixT[:, hd, :], ps[:, 4 + hd, :]).then_inc(retT_done, 1)

            def norm_std(n, t):
                act.wait_ge(var_done, n * NT + t + 1)
                nc.scalar.activation(col("std", t, 1), col("std", t, 1), ACT.Sqrt).then_inc(std_done, 1)

            def moe(L):
                act.wait_ge(logits_sub, L + 1)
                nc.scalar.activation(r_p, r_p, ACT.Exp).then_inc(logits_exp, 1)
                ysb = xs.rearrange("(b p) d -> b p d", p=P)

                def sigmoid(b, first=False):
                    act.wait_ge(gate_mm[L], b + 1)
                    if not first:
                        act.wait_ge(act_mul[L], b)
                    nc.scalar.activation(sig, ps[:, 0, :], ACT.Sigmoid).then_inc(sig_done[L], 1)

                def store(b, k, stores=None):
                    if stores is not None:
                        act.wait_ge(y_stored[L][k], stores)
                    for half in range(2):
                        act.wait_ge(down_mm[L], b * 2 + half + 1)
                        copy(yo[k][:, half * 512:(half + 1) * 512], ps[:, 2 + half, :]).then_inc(y_copied[L], 1)
                    act.wait_ge(y_copied[L], b * 2 + 2)
                    act.dma_start(ysb[bass.ds(b, 1)].rearrange("o p d -> p (o d)"), yo[k]).then_inc(y_stored[L][k], 16)

                sigmoid(0, first=True)
                sigmoid(1)
                act.wait_ge(scattered, (L + 1) * 16 * 2 * NT)
                store(0, 0)
                sigmoid(2)
                store(1, 1)
                with act.Fori(3, NE - 1, 2) as b:
                    for k in range(2):
                        sigmoid(b + k)
                        store(b + k - 1, k, (b - 1) * 8)
                sigmoid(NE - 1)
                store(NE - 2, 0, (NE - 2) * 8)
                store(NE - 1, 1, (NE - 2) * 8)
                act.wait_ge(table_done, L + 1)
                nx = act.value_load(tbl[0:1, T_NX:T_NX + 1], min_val=0, max_val=MAXX)
                with act.Fori(0, MAXX, 1) as j:
                    with act.If(j < nx):
                        sigmoid(j + NE)
                        store(j + NE, 0, (j + NE // 2) * 16)

            norm_std(0, 0)
            for t in range(1, NT + 1):
                if t < NT:
                    norm_std(0, t)
                turn_copies(1, t - 1)
            moe(0)

            def v_copies(t):
                for k in (2 * t, 2 * t + 1):
                    act.wait_ge(v_ps, k + 1)
                    copy(v1[:, t, (k % 2) * 512:(k % 2 + 1) * 512], ps[:, k, :]).then_inc(v_done, 1)

            norm_std(1, 0)
            turn_copies(2, 0)
            norm_std(1, 1)
            norm_std(1, 2)
            turn_copies(2, 1)
            v_copies(0)
            norm_std(1, 3)
            for t in range(2, NT + 1):
                if t < NT:
                    turn_copies(2, t)
                v_copies(t - 1)

            def stage(hd, f, first=False):
                act.wait_ge(hproj, hd * 4 + f + 1)
                if not first and f == 0:
                    act.wait_ge(prepped, hd)
                bank = ps[:, f % 2, :]
                if f in (0, 3):
                    a = {0: 0, 3: 2}[f]
                    copy(stg[:, a, :], bank)
                    nc.scalar.activation(stg[:, a + 1, :], bank, ACT.Sigmoid).then_inc(hproj_used, 1)
                else:
                    pos, neg = {1: (5, 6), 2: (4, 7)}[f]
                    nc.scalar.activation(stg[:, pos, :], bank, ACT.Sigmoid)
                    nc.scalar.activation(stg[:, neg, :], bank, ACT.Sigmoid, scale=-1.0).then_inc(hproj_used, 1)

            def scores(hd, last, first=False):
                if not first:
                    act.wait_ge(hpv_ps, hd)
                act.wait_ge(gram_ps, hd * 8 + 1)
                if first:
                    act.wait_ge(masks_in, 16)
                copy(diag, ps[:, 2, :].rearrange("p (c n) -> p c n", c=NT)).then_inc(diag_done, 1)
                if not last:
                    for f in range(3):
                        stage(hd + 1, f)
                act.wait_ge(off_ps, hd * 2 + 1)
                copy(neighbours, ps[:, 4, :].rearrange("p (a b n) -> p a b n", a=2, b=2)).then_inc(off_done, 1)
                act.wait_ge(off_ps, hd * 2 + 2)
                copy(attn[:, 0:2, 256:512], ps[:, 5, :].rearrange("p (a n) -> p a n", a=2))
                copy(attn[:, 2:4, 0:256], ps[:, 6, :].rearrange("p (a n) -> p a n", a=2)).then_inc(off_done, 1)
                if not last:
                    stage(hd + 1, 3)
                if not first:
                    act.wait_ge(sq_added, hd)
                act.wait_ge(hout_done, hd + 1)
                nc.scalar.activation(sqt, ps[:, 7, :], ACT.Square).then_inc(hsq_done, 1)

            for f in range(4):
                stage(0, f, first=True)
            scores(0, False, first=True)
            with act.Fori(1, HG - 1, 1) as hd:
                scores(hd, False)
            scores(HG - 1, True)
            act.wait_ge(rms_var, 1)
            nc.scalar.activation(col("rms"), col("rms"), ACT.Sqrt).then_inc(rms_std, 1)
            act.wait_ge(rms_done, 1)
            def scale_output(t):
                for k in (2 * t, 2 * t + 1):
                    act.wait_ge(op_ps, 2 * NT + k + 1)
                    if k >= 2:
                        act.wait_ge(op_added, k - 1)
                    nc.scalar.activation(ysc[:, k % 2, :], ps[:, k, :], ACT.Copy,
                                         scale=col("rms", t, 1)).then_inc(op_used, 1)

            scale_output(0)
            norm_std(2, 0)
            for t in range(1, NT + 1):
                if t < NT:
                    scale_output(t)
                    norm_std(2, t)
                turn_copies(3, t - 1)
            moe(1)
            for t in range(NT):
                norm_std(3, t)

        @block.vector
        def _(dve):
            v = nc.vector
            count = [0]

            def done(ins):
                count[0] += 1
                ins.then_inc(dve_order, 1)
                dve.wait_ge(dve_order, count[0])

            dve.wait_ge(tab_in, 64)
            pairs = [[DKR, 2 * HR], [2, DKR // 2]]
            tmp = [view(gelu_tmp, 256 * n, [[DKR // 2, 2 * HR], [1, DKR // 2]]) for n in range(4)]
            for t in range(NT):
                dve.wait_ge(proj_used, t + 1)
                if t > 0:
                    dve.wait_ge(rotated, t)
                x1, x2 = view(qk, t * 512, pairs), view(qk, t * 512 + 1, pairs)
                cos, sin = (view(rot[:], (2 * t + n) * (DKR // 2), [[0, 2 * HR], [1, DKR // 2]]) for n in range(2))
                v.tensor_tensor(tmp[0], x1, cos, ALU.mult)
                v.tensor_tensor(tmp[1], x2, sin, ALU.mult)
                v.tensor_tensor(tmp[2], x1, sin, ALU.mult)
                done(v.tensor_tensor(tmp[3], x2, cos, ALU.mult))
                v.tensor_tensor(x1, tmp[0], tmp[1], ALU.subtract)
                v.tensor_tensor(x2, tmp[2], tmp[3], ALU.add).then_inc(rotated, 1)
            dve.wait_ge(prmC, 1)
            lam = prm[:, R_LAM:R_LAM + 8]
            v.scalar_tensor_tensor(col("lam"), lam, -1.0, lam, ALU.mult, ALU.max).then_inc(lam_abs, 1)
            lb0, lb1 = prm[:, R_LB:R_LB + 8], prm[:, R_LB + 8:R_LB + 16]
            done(v.tensor_tensor(col("lbm"), lb0, lb1, ALU.max))
            v.tensor_tensor(col("lbe", 0, 8), lb0, col("lbm"), ALU.subtract)
            v.tensor_tensor(col("lbe", 8, 8), lb1, col("lbm"), ALU.subtract).then_inc(lb_sub, 1)
            for n in range(LRU_BLOCKS):
                dve.wait_ge(proj_used, 5 + n)

                def tap(j):
                    return prm[:, R_CW + 4 * j + n:R_CW + 4 * j + n + 1]

                done(v.tensor_scalar(xc[:, n, :], xrp[:, n, 0:T], tap(0), prm[:, R_CB + n:R_CB + n + 1],
                                     ALU.mult, ALU.add))
                for j in (1, 2, 3):
                    ins = v.scalar_tensor_tensor(xc[:, n, :], xrp[:, n, j:j + T], tap(j), xc[:, n, :], ALU.mult, ALU.add)
                    if j < 3:
                        done(ins)
                ins.then_inc(conv_done, 1)
            dve.wait_ge(lam_exp, 1)
            done(v.tensor_scalar(col("w"), col("lam"), 2.0, None, ALU.add))
            done(v.reciprocal(col("w"), col("w")))
            done(v.tensor_tensor(col("w"), col("w"), col("lam"), ALU.mult))
            done(v.tensor_tensor(col("w2"), col("w"), col("w"), ALU.mult))
            done(v.tensor_scalar(col("p"), col("w2"), 1.0 / 15, None, ALU.mult))
            for n in (13, 11, 9, 7, 5, 3):
                done(v.scalar_tensor_tensor(col("p"), col("p"), 1.0 / n, col("w2"), ALU.add, ALU.mult))
            done(v.scalar_tensor_tensor(col("p"), col("p"), 1.0, col("w"), ALU.add, ALU.mult))
            done(v.tensor_scalar(col("w2"), lam, -1.0, 0.0, ALU.mult, ALU.max))
            done(v.scalar_tensor_tensor(col("p"), col("p"), 2.0, col("w2"), ALU.mult, ALU.add))
            v.tensor_scalar(col("negc"), col("p"), -8.0, None, ALU.mult)
            v.tensor_scalar(col("c"), col("p"), 8.0, None, ALU.mult).then_inc(lam_c, 1)
            dve.wait_ge(lb_exp, 1)
            done(v.tensor_tensor(col("lbm"), col("lbe", 0, 8), col("lbe", 8, 8), ALU.add))
            done(v.reciprocal(col("lbm"), col("lbm")))
            done(v.tensor_tensor(col("lb"), col("lbe", 8, 8), col("lbm"), ALU.mult))
            done(v.tensor_scalar(col("olb"), col("lb"), -1.0, 1.0, ALU.mult, ALU.add))

            for t in range(NT):
                dve.wait_ge(qkT_ps, t + 1)
                v.tensor_copy(qkT[:, :, t * P:(t + 1) * P], ps[:, t, :].rearrange("p (c n) -> p c n", c=4)
                              ).then_inc(qkT_done, 1)
            for i in range(NT):
                dve.wait_ge(g_sigm, i + 1)
                v.tensor_tensor(g0[:, i, :], g0[:, i, :], ps[:, 4 + i, :], ALU.mult).then_inc(g_used, 1)

            for z in range(2):
                dve.wait_ge(gate_done, 16)
                v.tensor_tensor(IG[z], IG[z], xc, ALU.mult)
                dve.wait_ge(a_done, z + 1)
                done(v.tensor_tensor(TMP, A_, A_, ALU.mult))
                dve.wait_ge(tanh_done, z + 1)
                v.scalar_tensor_tensor(TMP, TMP, 1.0, R[z], ALU.add, ALU.mult).then_inc(ratio, 1)
                dve.wait_ge(ratio_sqrt, z + 1)
                dve.wait_ge(ratio, z + 1)
                done(v.tensor_tensor(IG[z], IG[z], TMP, ALU.mult))
                for n in range(LRU_BLOCKS):
                    if z == 0:
                        o, a, b = R[0][:, n, :], A_[:, n, :], IG[0][:, n, :]
                    else:
                        o, a, b = (view(buf, n * T + T - 1, [[-1, T]]) for buf in (R[1], A_, IG[1]))
                    ins = v.tensor_tensor_scan(o, a, b, 0.0, ALU.mult, ALU.add)
                ins.then_inc(scanned, 1)
            dve.wait_ge(scanned, 2)
            done(v.tensor_tensor(R[0], R[0], R[1], ALU.add))
            dve.wait_ge(gelu_done, 1)
            dve.wait_ge(proj, 20)
            v.tensor_tensor(mixT[:, 4:8, :], R[0], gr, ALU.mult).then_inc(lru_done, 1)

            def head_statistics(hd):
                dve.wait_ge(pv_ps, hd + 1)
                for t in range(NT):
                    last = v.bn_stats(col("rst", 6 * t, 6), ps[:, 4 + hd, t * P:(t + 1) * P])
                done(last)
                for t in range(NT):
                    last = v.bn_aggr(col("rag", 2 * (hd * NT + t), 2), col("rst", 6 * t, 6))
                done(last)
                v.tensor_scalar(col("rvar", hd * NT, NT), view(col("rag"), 2 * hd * NT + 1, [[2, NT]]), LN_EPS, None,
                                ALU.add).then_inc(ret_var, 1)

            def head_norm(hd):
                dve.wait_ge(ret_std, hd + 1)
                done(v.reciprocal(col("rvar", hd * NT, NT), col("rvar", hd * NT, NT)))
                for t in range(NT):
                    n = hd * NT + t
                    last = v.tensor_scalar(ret[:, t, hd * P:(hd + 1) * P], ps[:, 4 + hd, t * P:(t + 1) * P],
                                           col("rag", 2 * n, 1), col("rvar", n, 1), ALU.subtract, ALU.mult)
                done(last)
                v.tensor_tensor(ret[:, :, hd * P:(hd + 1) * P], ret[:, :, hd * P:(hd + 1) * P],
                                g0[:, :, hd * P:(hd + 1) * P], ALU.mult).then_inc(ret_done, 1)

            for hd in range(HR + 2):
                if hd >= 2:
                    head_statistics(hd - 2)
                if hd < HR:
                    if hd >= 2:
                        dve.wait_ge(pv_ps, hd - 1)
                    for j in range(NT):
                        dve.wait_ge(score_ps, hd * NT + j + 1)
                        at = (NT - 1 - j) * P
                        v.tensor_tensor(prob[hd % 2][:, j, :], ps[:, j, :], decay[:, hd, at:at + T], ALU.mult
                                        ).then_inc(prob_done, 1)
                if hd >= 2:
                    head_norm(hd - 2)

            def standardise(n, t):
                for half in range(2):
                    last = v.bn_stats(col("st", 6 * half, 6), h[:, t, half * 512:(half + 1) * 512])
                done(last)
                done(v.bn_aggr(col("ag", 2 * t, 2), col("st")))
                v.tensor_scalar(col("std", t, 1), col("ag", 2 * t + 1, 1), LN_EPS, None, ALU.add).then_inc(var_done, 1)
                dve.wait_ge(std_done, n * NT + t + 1)
                done(v.reciprocal(col("rst1", t, 1), col("std", t, 1)))
                ins = v.tensor_scalar(h[:, t, :], h[:, t, :], col("ag", 2 * t, 1), col("rst1", t, 1),
                                      ALU.subtract, ALU.mult)
                if n == 3 and t < NT - 1:
                    ins.then_inc(standard, 1)
                    return
                done(ins)
                if t == (NT - 1 if n == 3 else 0):
                    dve.wait_ge(lnp_in, 32 * (n + 1))
                done(v.tensor_tensor(h[:, t, :], h[:, t, :], lnw, ALU.mult))
                if n == 3:
                    dve.wait_ge(ln_done, n * NT + t)
                v.tensor_tensor(h[:, t, :], h[:, t, :], lnb, ALU.add).then_inc(ln_done, 1)

            def norm(n, add):
                for t in range(NT):
                    add(t)
                    standardise(n, t)

            def add_mixer(L):
                def add(t):
                    for half in range(2):
                        k = 2 * t + half
                        hh = h[:, t, half * 512:(half + 1) * 512]
                        if L == 0:
                            dve.wait_ge(op_ps, k + 1)
                            v.scalar_tensor_tensor(hh, hh, ALPHA, ps[:, k, :], ALU.mult, ALU.add
                                                   ).then_inc(op_used, 1)
                        else:
                            dve.wait_ge(op_used, 2 * NT + k + 1)
                            v.scalar_tensor_tensor(hh, hh, ALPHA, ysc[:, k % 2, :], ALU.mult, ALU.add
                                                   ).then_inc(op_added, 1)
                    dve.wait_ge((op_used, op_added)[L], 2 * t + 2)
                return add

            def add_moe(L):
                def add(t):
                    dve.wait_ge(gathered[t], (L + 1) * 32)
                    if t == 0:
                        dve.wait_ge(h_scaled, L + 1)
                    for k in range(2):
                        done(v.scalar_tensor_tensor(h[:, t, :], Yg[:, 2 * t + k, :], gts[:, t, k:k + 1], h[:, t, :],
                                                    ALU.mult, ALU.add))
                return add

            def rank(rk, val, n):
                gt, ge = (a[:, 0:n * EPG * EPG].rearrange("p (n j i) -> p n j i", j=EPG, i=EPG) for a in (r_gt, r_ge))
                mine = view(val, 0, [[EPG, n], [1, EPG], [0, EPG]])
                other = view(val, 0, [[EPG, n], [0, EPG], [1, EPG]])
                before = view(iota[:], P, [[0, n], [EPG, EPG], [1, EPG]])
                v.tensor_tensor(gt, other, mine, ALU.is_gt)
                done(v.tensor_tensor(ge, other, mine, ALU.is_ge))
                done(v.tensor_tensor(ge, ge, before, ALU.mult))
                done(v.tensor_tensor(gt, gt, ge, ALU.max))
                done(v.tensor_reduce(rk.rearrange("p (n j) -> p n j", j=EPG), gt, AX.X, ALU.add))

            def route(L):
                def by_token(a):
                    return a.rearrange("p (t e) -> p t e", t=NT)

                def per_token(a):
                    return view(a, 0, [[1, NT], [0, NE]])

                dve.wait_ge(logits_ps, (L + 1) * NT)
                lg = by_token(ps[:, 0, 0:NT * NE])
                v.memset(r_msk5[:, NT * NE:], 0.0)
                done(v.tensor_reduce(r_t4, lg, AX.X, ALU.max))
                v.tensor_tensor(by_token(r_p), lg, per_token(r_t4), ALU.subtract).then_inc(logits_sub, 1)
                dve.wait_ge(logits_exp, L + 1)
                done(v.tensor_reduce(r_t4, by_token(r_p), AX.X, ALU.add))
                done(v.reciprocal(r_t4, r_t4))
                done(v.tensor_tensor(by_token(r_p), by_token(r_p), per_token(r_t4), ALU.mult))
                rank(r_rk, r_p, NT * NG)
                done(v.tensor_scalar(r_sel, r_rk, 2.0, None, ALU.is_lt))
                done(v.tensor_tensor(r_x, r_p, r_sel, ALU.mult))
                done(v.tensor_reduce(r_grp, r_x.rearrange("p (g e) -> p g e", e=EPG), AX.X, ALU.add))
                rank(r_grk, r_grp, NT)
                done(v.tensor_scalar(r_grk, r_grk, 1.0, None, ALU.is_lt))
                v.tensor_tensor(r_msk.rearrange("p (g e) -> p g e", e=EPG), r_sel.rearrange("p (g e) -> p g e", e=EPG),
                                view(r_grk, 0, [[1, NT * NG], [0, EPG]]), ALU.mult).then_inc(mask_done, 1)
                dve.wait_ge(mask_done, L + 1)
                done(v.tensor_tensor(r_x, r_p, r_msk, ALU.mult))
                done(v.tensor_reduce(r_t4, by_token(r_x), AX.X, ALU.add))
                done(v.reciprocal(r_t4, r_t4))
                done(v.tensor_tensor(by_token(r_x), by_token(r_x), per_token(r_t4), ALU.mult))
                done(v.tensor_scalar(r_sel, r_msk, -BIG, BIG, ALU.mult, ALU.add))
                dve.wait_ge(cum_ps, L + 1)
                r_cnt, ranks = ps[:, 1, NT * NE:(NT + 1) * NE], by_token(ps[:, 1, 0:NT * NE])
                done(v.tensor_scalar(r_nbk, r_cnt, float(P), None, ALU.is_gt))
                for k in range(2, NT):
                    done(v.scalar_tensor_tensor(r_nbk, r_cnt, float(k * P), r_nbk, ALU.is_gt, ALU.add))
                done(v.tensor_tensor_scan(r_end, ones[:, 0:NE], r_nbk, 0.0, ALU.mult, ALU.add))
                done(v.tensor_tensor(r_skip, r_end, r_nbk, ALU.subtract))
                done(v.tensor_tensor(r_skip, r_skip, iota[:, 0:NE], ALU.subtract))
                v.tensor_scalar(by_token(r_over), ranks, float(P), float(P), ALU.is_ge, ALU.mult)
                done(v.tensor_scalar(r_skip, r_skip, float(NE - 1), None, ALU.add))
                v.scalar_tensor_tensor(by_token(r_d), view(iota[:], 0, [[0, NT], [1, NE]]), float(P), ranks,
                                       ALU.mult, ALU.add)
                done(v.tensor_tensor(by_token(r_over), by_token(r_over), view(r_skip, 0, [[0, NT], [1, NE]]), ALU.mult))
                done(v.tensor_tensor(r_d, r_d, r_over, ALU.add))
                done(v.tensor_tensor(r_d, r_d, r_msk, ALU.mult))
                done(v.tensor_tensor(r_sel, r_sel, r_d, ALU.add))
                slots = ((r_sel, r_t4), (r_d, r_grk[:, 0:NT]))
                v.tensor_reduce(r_t4, by_token(r_sel), AX.X, ALU.min)
                done(v.tensor_reduce(r_grk[:, 0:NT], by_token(r_d), AX.X, ALU.max))
                for k, (_, slot) in enumerate(slots):
                    ins = v.tensor_copy(dst[:, :, k], slot)
                ins.then_inc(slots_done, 1)
                for t in range(NT):
                    ins = v.tensor_scalar(first_sel[:, t, :], iota[:, 0:P], r_sel[:, t * NE:t * NE + 1], None, ALU.is_equal)
                ins.then_inc(sel_done, 1)
                for k, (d, slot) in enumerate(slots):
                    done(v.tensor_tensor(by_token(r_rk), by_token(d), per_token(slot), ALU.is_equal))
                    done(v.tensor_tensor(r_rk, r_rk, r_x, ALU.mult))
                    done(v.tensor_reduce(gts[:, :, k], by_token(r_rk), AX.X, ALU.add))
                b3 = view(r_blk[0:1], 0, [[NE, MAXX], [1, NE]])
                done(v.tensor_tensor(b3, view(iota[0:1], 0, [[1, MAXX], [0, NE]]), view(r_end[0:1], 0, [[0, MAXX], [1, NE]]),
                                     ALU.is_ge))
                done(v.memset(r_tb[0:1], 0.0))
                done(v.tensor_reduce(r_tb[0:1, 0:MAXX], b3, AX.X, ALU.add))
                done(v.tensor_scalar(r_tb[0:1, 0:MAXX], r_tb[0:1, 0:MAXX], float(NE - 1), None, ALU.min))
                v.tensor_copy(r_tb[0:1, T_NX:T_NX + 1], r_end[0:1, NE - 1:NE])
                done(v.tensor_scalar(r_tb[0:1, T_STORES:T_STORES + 1], r_end[0:1, NE - 1:NE], float(NE // 2), 16.0,
                                     ALU.add, ALU.mult))
                v.tensor_copy(tbl[:], r_tb[0:1]).then_inc(table_done, 1)

            def moe(L):

                def copy_rows(b):
                    for half in range(2):
                        dve.wait_ge(xgT_ps[L], b * 2 + half + 1)
                        v.tensor_copy(xgT[:, half * 4:half * 4 + 4, :],
                                      ps[:, 4 + half, :].rearrange("p (c n) -> p c n", c=4)).then_inc(xgT_done[L], 1)

                def hidden(b, first=False):
                    dve.wait_ge(sig_done[L], b + 1)
                    v.tensor_tensor(gs, sig, ps[:, 0, :], ALU.mult).then_inc(act_mul[L], 1)
                    dve.wait_ge(act_mul[L], b + 1)
                    dve.wait_ge(up_mm[L], b + 1)
                    if not first:
                        dve.wait_ge(hidT_ps[L], b)
                    v.tensor_tensor(hid, gs, ps[:, 1, :], ALU.mult).then_inc(hid_done[L], 1)

                def copy_hidden(b):
                    dve.wait_ge(hidT_ps[L], b + 1)
                    v.tensor_copy(hidT, ps[:, 6, :].rearrange("p (c n) -> p c n", c=NF)).then_inc(hidT_done[L], 1)

                copy_rows(0)
                hidden(0, first=True)
                copy_rows(1)
                copy_hidden(0)
                with dve.Fori(1, NE - 1, 1) as b:
                    hidden(b)
                    copy_rows(b + 1)
                    copy_hidden(b)
                hidden(NE - 1)
                copy_hidden(NE - 1)
                dve.wait_ge(table_done, L + 1)
                nx = dve.value_load(tbl[0:1, T_NX:T_NX + 1], min_val=0, max_val=MAXX)
                with dve.Fori(0, MAXX, 1) as j:
                    with dve.If(j < nx):
                        copy_rows(j + NE)
                        hidden(j + NE)
                        copy_hidden(j + NE)

            norm(0, add_mixer(0))
            dve.wait_ge(xs_zeroed, 16 * 4)
            route(0)
            moe(0)
            norm(1, add_moe(0))

            def output(hd):
                dve.wait_ge(hpv_ps, hd + 1)
                v.tensor_tensor(OG[:, bass.ds(hd, 1), :].rearrange("p o t -> p (o t)"), ps[:, 7, :], sg, ALU.mult
                                ).then_inc(hout_done, 1)

            def prepare(hd, first=False):
                dve.wait_ge(hproj_used, hd * 4 + 3)
                if not first:
                    dve.wait_ge(off_ps, hd * 2)
                lb, olb, nw = (a[:, bass.ds(hd, 1)] for a in (col("lb"), col("olb"), prm[:, R_NW:R_NW + HG]))
                v.tensor_scalar(FF, stg[:, 4:6, :], olb, lb, ALU.mult, ALU.add)
                v.tensor_scalar(K2, stg[:, 6:8, :], olb, None, ALU.mult)
                v.scalar_tensor_tensor(qs, stg[:, 0, :], float(P) ** -0.5, stg[:, 1, :], ALU.mult, ALU.mult
                                       ).then_inc(prep_in, 1)
                if not first:
                    output(hd - 1)
                    dve.wait_ge(hout_done, hd)
                dve.wait_ge(hproj_used, hd * 4 + 4)
                v.scalar_tensor_tensor(sg, stg[:, 2, :], nw, stg[:, 3, :], ALU.mult, ALU.mult)
                dve.wait_ge(prep_in, hd + 1)
                v.tensor_tensor(Q2, view(qs, 0, [[0, 2], [1, T]]), FF, ALU.mult)
                v.tensor_tensor(ksum, K2[:, 0, :], K2[:, 1, :], ALU.add).then_inc(prepped, 1)

            def segment_products(s):
                if s == 1:
                    return FF, 0, T
                return TL, 2 * T - 4 * T // s, T // s

            def update(hd, u):
                s = 1 << (u - 1)
                n = T // (2 * s)
                if u == 1:
                    dve.wait_ge(prepped, hd + 1)
                else:
                    dve.wait_ge(updated, hd * 8 + u - 1)
                    dve.wait_ge(level_done, hd * LEVELS + u - 1)
                src, at, step = segment_products(s)
                if u < 8:
                    to, at2, step2 = segment_products(2 * s)
                    v.tensor_tensor(view(to, at2, [[step2, 2], [1, n]]), view(src, at, [[step, 2], [2, n]]),
                                    view(src, at + 1, [[step, 2], [2, n]]), ALU.mult)
                if u < 8:
                    dve.wait_ge(gram_ps, hd * 8 + u + 1)
                else:
                    dve.wait_ge(off_ps, hd * 2 + 1)
                q, k = mixed(Q2, s, 0, T), mixed(K2, s, 0, T)
                v.tensor_tensor(k, k,
                                view(src, at + step + 1, [[2, n], [-(step + 1), 2], [0, s]]), ALU.mult
                                ).then_inc(keys_updated, 1)
                v.tensor_tensor(q, q,
                                view(src, at + 1, [[2, n], [step - 1, 2], [0, s]]), ALU.mult).then_inc(updated, 1)

            def pick(hd, level):
                if level == 1:
                    dve.wait_ge(masks_in, 16)
                    dve.wait_ge(diag_done, hd + 1)
                v.copy_predicated(diag, view(masks, (level - 1) * P, [[0, NT], [1, P]]),
                                  ps[:, 2 + level % 2, :].rearrange("p (c n) -> p c n", c=NT)).then_inc(level_done, 1)

            def head(hd, first=False):
                prepare(hd, first)
                for u in range(1, 9):
                    update(hd, u)
                    if u < 8:
                        pick(hd, u)

            dve.wait_ge(masks_in, 16)
            head(0, first=True)
            with dve.Fori(1, HG, 1) as hd:
                head(hd)
            output(HG - 1)
            dve.wait_ge(ssq_ps, 1)
            v.tensor_scalar(col("rms"), ps[:, 7, 0:NT], 1.0 / D, RMS_EPS, ALU.mult, ALU.add).then_inc(rms_var, 1)
            dve.wait_ge(rms_std, 1)
            v.reciprocal(col("rms"), col("rms")).then_inc(rms_done, 1)
            norm(2, add_mixer(1))
            route(1)
            moe(1)
            norm(3, add_moe(1))

        @block.gpsimd
        def _(pool):
            pool.memset(zero, 0.0).then_inc(zero_set, 1)
            pool.memset(xrp[:, :, 0:2], 0.0)
            pool.memset(xrp[:, :, T + 2:PADC], 0.0).then_inc(pads_set, 1)
            pool.wait_ge(rotated, NT)
            pool.wait_ge(proj_used, 12)
            pool.tensor_tensor(gelu_tmp, gr, gr, ALU.mult).then_inc(pool_order, 1)
            pool.wait_ge(pool_order, 1)
            pool.tensor_scalar(gelu_tmp, gelu_tmp, 0.044715, 1.0, ALU.mult, ALU.add).then_inc(pool_order, 1)
            pool.wait_ge(pool_order, 2)
            pool.tensor_tensor(gelu_tmp, gelu_tmp, gr, ALU.mult).then_inc(gelu_arg, 1)
            pool.wait_ge(gelu_sig, 1)
            pool.tensor_tensor(gr, gr, gelu_tmp, ALU.mult).then_inc(gelu_done, 1)

            def last_affine():
                pool.wait_ge(lnp_in, 32 * 4)
                for t in range(NT - 1):
                    pool.wait_ge(standard, t + 1)
                    pool.tensor_tensor(h[:, t, :], h[:, t, :], lnw, ALU.mult).then_inc(affine, 1)
                    pool.wait_ge(affine, t + 1)
                    pool.tensor_tensor(h[:, t, :], h[:, t, :], lnb, ALU.add).then_inc(ln_done, 1)

            def moe(L):
                pool.wait_ge(slots_done, L + 1)
                pool.wait_ge(xs_zeroed, 16 * 4)
                for t in range(NT):
                    for k in range(2):
                        pool.indirect_dma_start(xs, bass.IndirectOffsetOnAxis(ap=dst[:, t, k:k + 1], axis=0),
                                                h[:, t, :], None).then_inc(scattered, 16)
                pool.wait_ge(scattered, (L + 1) * 16 * 2 * NT)
                pool.wait_ge(xgT_ps[L], 2)
                pool.tensor_scalar(h[:], h[:], ALPHA, None, ALU.mult).then_inc(h_scaled, 1)
                pool.wait_ge(table_done, L + 1)
                stores = pool.value_load(tbl[0:1, T_STORES:T_STORES + 1], min_val=16 * (NE // 2),
                                         max_val=16 * (NE // 2 + MAXX))
                pool.wait_ge(y_stored[L][1], 16 * (NE // 2))
                pool.wait_ge(y_stored[L][0], stores)
                for t in range(NT):
                    for k in range(2):
                        pool.indirect_dma_start(Yg[:, 2 * t + k, :], None, xs,
                                                bass.IndirectOffsetOnAxis(ap=dst[:, t, k:k + 1], axis=0)
                                                ).then_inc(gathered[t], 16)

            moe(0)
            pool.wait_ge(v_done, 2 * NT)
            pool.memset(SQ, 0.0).then_inc(sq_zero, 1)

            def head(hd, first=False):
                pool.wait_ge(v_done, 2 * NT)
                if not first:
                    pool.wait_ge(hpv_ps, hd)
                pool.tensor_copy(vh, v1[:, :, bass.ds(hd * P, P)]).then_inc(vh_done, 1)
                for level in range(1, LEVELS + 1):
                    s = 1 << (level - 1)
                    if level == 1:
                        pool.wait_ge(prepped, hd + 1)
                    else:
                        pool.wait_ge(keys_updated, hd * 8 + level - 1)
                    if level >= 3:
                        pool.wait_ge(gram_ps, hd * 8 + level - 1)
                    pool.tensor_tensor(view(km[level % 2], 0, [[2 * s, T // (2 * s)], [s, 2], [1, s]]),
                                       mixed(K2, s, 0, T), view(ones, 0, [[0, T // (2 * s)], [0, 2], [0, s]]), ALU.mult
                                       ).then_inc(keys_mixed, 1)
                pool.wait_ge(hsq_done, hd + 1)
                if first:
                    pool.wait_ge(sq_zero, 1)
                else:
                    pool.wait_ge(sq_added, hd)
                pool.tensor_tensor(SQ, SQ, sqt, ALU.add).then_inc(sq_added, 1)

            head(0, first=True)
            with pool.Fori(1, HG, 1) as hd:
                head(hd)
            moe(1)
            last_affine()


_INS = ['x', 'w_in_even', 'w_out_even', 'lru_conv_w', 'lru_conv_b', 'lru_gate_w', 'lru_gate_b', 'lru_lambda',
        'w_in_odd', 'w_out_odd', 'hg_lower_bounds', 'hg_norm_w', 'ln_w', 'ln_b', 'router_w',
        'moe_w_gate', 'moe_w_up', 'moe_w_down']


def kernel(**inputs):
    import concourse.bacc as bacc
    from concourse.bass_utils import run_bass_kernel_spmd

    nc = bacc.Bacc("TRN2", target_bir_lowering=False, num_devices=1)
    arrays, args = {}, []
    everything = [(n, inputs[n]) for n in _INS] + sorted(constants().items())
    handles = {}
    for name, a in everything:
        a = np.ascontiguousarray(a)
        arrays[name] = a
        handles[name] = nc.dram_tensor(name, a.shape, mybir.dt.from_np(a.dtype), kind="ExternalInput").ap()
    handles["out"] = nc.dram_tensor("out", (1, T, D), F32, kind="ExternalOutput").ap()
    encoder_kernel(nc, **handles)
    r = run_bass_kernel_spmd(nc, [arrays], core_ids=[0])
    return r.results[0]["out"]
```
